# Optimizing a Trainium2 kernel written in Bass

```python
import jax, jax.numpy as jnp
from jax import lax
import numpy as np

D_MODEL = 2048
BATCH = 1
SEQ = 256
DEPTH = 1

HEAD_DIM = 128
ROPE_THETA = 10000.0
Q_BLOCK = 128
LN_EPS = 1e-5
DEEPNORM_ALPHA = (2 * DEPTH) ** 0.25
DEEPNORM_BETA = (8 * DEPTH) ** -0.25
FFN_HIDDEN = 256 * ((8 * D_MODEL // 3 + 255) // 256)

NSA_HEADS = 8
NSA_KV_GROUPS = 2
NSA_HPG = NSA_HEADS // NSA_KV_GROUPS
CMP_BLOCK = 32
CMP_STRIDE = 16
CMP_HIDDEN = 2 * HEAD_DIM
SEL_BLOCK = 64
SEL_TOPK = 16
WIN = 512

DIL_PATTERNS = ((128, 1), (512, 4), (2048, 16))
N_DIL = len(DIL_PATTERNS)
DIL_HPG = 4
DIL_HEADS = N_DIL * DIL_HPG

NSA_Q_W = NSA_HEADS * HEAD_DIM
NSA_KV_W = NSA_KV_GROUPS * HEAD_DIM
NSA_GATE_W = NSA_HEADS * 3
DIL_W = DIL_HEADS * HEAD_DIM
IN_SIZES = (NSA_Q_W, NSA_KV_W, NSA_KV_W, NSA_KV_W, NSA_KV_W, NSA_KV_W, NSA_KV_W, NSA_GATE_W,
            DIL_W, DIL_W, DIL_W, D_MODEL, D_MODEL)
IN_WIDTH = sum(IN_SIZES)
BRANCH_A_W = NSA_HEADS * HEAD_DIM
BRANCH_B_W = DIL_HPG * HEAD_DIM

kernel_name = "hybrid_nsa_dilated_macaron_deepnorm"

def _layer_norm(x, g, b):
    xf = x.astype(jnp.float32)
    mu = jnp.mean(xf, -1, keepdims=True)
    var = jnp.mean(jnp.square(xf - mu), -1, keepdims=True)
    y = (xf - mu) * lax.rsqrt(var + LN_EPS) * g.astype(jnp.float32) + b.astype(jnp.float32)
    return y.astype(x.dtype)

def _swiglu(x, w_gate, w_up, w_down):
    return (jax.nn.silu(x @ w_gate) * (x @ w_up)) @ w_down

def _rope(x):
    s = x.shape[-2]
    inv = ROPE_THETA ** (-jnp.arange(0, HEAD_DIM, 2, dtype=jnp.float32) / HEAD_DIM)
    ang = jnp.arange(s, dtype=jnp.float32)[:, None] * inv[None, :]
    cos, sin = jnp.cos(ang), jnp.sin(ang)
    x1, x2 = jnp.split(x.astype(jnp.float32), 2, axis=-1)
    return jnp.concatenate([x1 * cos - x2 * sin, x2 * cos + x1 * sin], -1).astype(x.dtype)

def _masked_softmax(s, mask):
    s = jnp.where(mask, s, -jnp.inf)
    m = jnp.max(s, -1, keepdims=True)
    m = jnp.where(jnp.isfinite(m), m, 0.0)
    e = jnp.exp(s - m)
    d = jnp.sum(e, -1, keepdims=True)
    return e / jnp.where(d > 0, d, 1.0)

def _compress(t, pos, w1, w2):
    s = t.shape[2]
    n_cmp = (s - CMP_BLOCK) // CMP_STRIDE + 1
    idx = jnp.arange(n_cmp)[:, None] * CMP_STRIDE + jnp.arange(CMP_BLOCK)[None, :]
    blk = t[:, :, idx] + pos.astype(t.dtype)
    blk = blk.reshape(blk.shape[:3] + (CMP_BLOCK * HEAD_DIM,))
    return jax.nn.gelu(blk @ w1) @ w2

def _nsa(q, k_cmp, v_cmp, k_slc, v_slc, k_win, v_win, gate_logits,
         ck_pos, ck_w1, ck_w2, cv_pos, cv_w1, cv_w2):
    b, _, s, _ = q.shape
    G, HPG, dh = NSA_KV_GROUPS, NSA_HPG, HEAD_DIM
    scale = dh ** -0.5
    q_plain = q.reshape(b, G, HPG, s, dh)
    q_rot = _rope(q).reshape(b, G, HPG, s, dh)
    kc = _compress(k_cmp, ck_pos, ck_w1, ck_w2)
    vc = _compress(v_cmp, cv_pos, cv_w1, cv_w2)
    n_cmp = kc.shape[2]
    n_sel = s // SEL_BLOCK
    top = min(SEL_TOPK, n_sel)
    cmp_end = jnp.arange(n_cmp) * CMP_STRIDE + CMP_BLOCK - 1
    c0 = jnp.arange(n_cmp) * CMP_STRIDE
    s0 = jnp.arange(n_sel) * SEL_BLOCK
    overlap = jnp.clip(jnp.minimum(c0[:, None] + CMP_BLOCK, s0[None, :] + SEL_BLOCK)
                       - jnp.maximum(c0[:, None], s0[None, :]), 0)
    cmp_to_sel = overlap.astype(jnp.float32) / CMP_STRIDE
    ks = _rope(k_slc).reshape(b, G, n_sel, SEL_BLOCK, dh)
    vs = v_slc.reshape(b, G, n_sel, SEL_BLOCK, dh)
    pad = ((0, 0), (0, 0), (WIN, 0), (0, 0))
    kw = jnp.pad(_rope(k_win), pad)
    vw = jnp.pad(v_win, pad)
    gates = jax.nn.sigmoid(gate_logits.astype(jnp.float32)).reshape(b, s, G, HPG, 3).transpose(0, 2, 3, 1, 4)
    bi = jnp.arange(b)[:, None, None, None]
    gi = jnp.arange(G)[None, :, None, None]
    blk_id = jnp.arange(n_sel)

    def block(i):
        start = i * Q_BLOCK
        t = start + jnp.arange(Q_BLOCK)
        qc = lax.dynamic_slice_in_dim(q_plain, start, Q_BLOCK, axis=3)
        qr = lax.dynamic_slice_in_dim(q_rot, start, Q_BLOCK, axis=3)
        sc = jnp.einsum('bghqd,bgnd->bghqn', qc, kc).astype(jnp.float32) * scale
        pc = _masked_softmax(sc, cmp_end[None, :] <= t[:, None])
        o_cmp = jnp.einsum('bghqn,bgnd->bghqd', pc.astype(vc.dtype), vc)
        imp = jnp.einsum('bghqn,nj->bgqj', pc, cmp_to_sel)
        cur = t // SEL_BLOCK
        valid = blk_id[None, :] <= cur[:, None]
        forced = (blk_id[None, :] == 0) | (blk_id[None, :] == cur[:, None]) | (blk_id[None, :] == cur[:, None] - 1)
        imp = jnp.where(valid, jnp.where(forced, jnp.inf, imp), -jnp.inf)
        _, top_idx = lax.top_k(imp, top)
        k_sel = ks[bi, gi, top_idx].reshape(b, G, Q_BLOCK, top * SEL_BLOCK, dh)
        v_sel = vs[bi, gi, top_idx].reshape(b, G, Q_BLOCK, top * SEL_BLOCK, dh)
        kpos = (top_idx[..., None] * SEL_BLOCK + jnp.arange(SEL_BLOCK)).reshape(b, G, Q_BLOCK, top * SEL_BLOCK)
        sel_mask = kpos <= t[:, None]
        ssl = jnp.einsum('bghqd,bgqkd->bghqk', qr, k_sel).astype(jnp.float32) * scale
        ps = _masked_softmax(ssl, sel_mask[:, :, None])
        o_slc = jnp.einsum('bghqk,bgqkd->bghqd', ps.astype(v_sel.dtype), v_sel)
        kwb = lax.dynamic_slice_in_dim(kw, start, Q_BLOCK + WIN, axis=2)
        vwb = lax.dynamic_slice_in_dim(vw, start, Q_BLOCK + WIN, axis=2)
        wpos = start - WIN + jnp.arange(Q_BLOCK + WIN)
        wmask = (wpos[None, :] >= 0) & (wpos[None, :] <= t[:, None]) & (wpos[None, :] > t[:, None] - WIN)
        sw = jnp.einsum('bghqd,bgkd->bghqk', qr, kwb).astype(jnp.float32) * scale
        pw = _masked_softmax(sw, wmask)
        o_win = jnp.einsum('bghqk,bgkd->bghqd', pw.astype(vwb.dtype), vwb)
        g = lax.dynamic_slice_in_dim(gates, start, Q_BLOCK, axis=3)
        o = g[..., 0:1] * o_cmp + g[..., 1:2] * o_slc + g[..., 2:3] * o_win
        return o.astype(q.dtype)

    out = lax.map(block, jnp.arange(s // Q_BLOCK))
    return out.transpose(1, 0, 4, 2, 3, 5).reshape(b, s, NSA_HEADS * dh)

def _dilated(q, k, v):
    b, _, s, dh = q.shape
    scale = dh ** -0.5
    qg = q.reshape(b, N_DIL, DIL_HPG, s, dh)
    kg = k.reshape(b, N_DIL, DIL_HPG, s, dh)
    vg = v.reshape(b, N_DIL, DIL_HPG, s, dh)

    def block(i):
        start = i * Q_BLOCK
        t = start + jnp.arange(Q_BLOCK)
        qb = lax.dynamic_slice_in_dim(qg, start, Q_BLOCK, axis=3)
        outs, lses = [], []
        for gidx, (win, dil) in enumerate(DIL_PATTERNS):
            n_keys = win // dil + 1
            kpos = t[:, None] - dil * jnp.arange(n_keys)[None, :]
            idx = jnp.maximum(kpos, 0)
            kk = kg[:, gidx][:, :, idx]
            vv = vg[:, gidx][:, :, idx]
            sc = jnp.einsum('bhqd,bhqkd->bhqk', qb[:, gidx], kk).astype(jnp.float32) * scale
            sc = jnp.where(kpos >= 0, sc, -jnp.inf)
            lse = jax.nn.logsumexp(sc, axis=-1)
            p = jnp.exp(sc - lse[..., None])
            outs.append(jnp.einsum('bhqk,bhqkd->bhqd', p.astype(vv.dtype), vv).astype(jnp.float32))
            lses.append(lse)
        w = jax.nn.softmax(jnp.stack(lses), axis=0)
        o = jnp.sum(w[..., None] * jnp.stack(outs), axis=0)
        return o.astype(q.dtype)

    out = lax.map(block, jnp.arange(s // Q_BLOCK))
    return out.transpose(1, 0, 3, 2, 4).reshape(b, s, DIL_HPG * dh)

def _mixer(h, w_in, ck_pos, ck_w1, ck_w2, cv_pos, cv_w1, cv_w2, w_branch_a, w_branch_b, w_o):
    b, s, _ = h.shape
    proj = h @ w_in
    points, acc = [], 0
    for size in IN_SIZES[:-1]:
        acc += size
        points.append(acc)
    (q_a, kc, vc, ksl, vsl, kwn, vwn, g_nsa, q_b, k_b, v_b, g_a, g_b) = jnp.split(proj, points, axis=-1)

    def heads(t, n):
        return t.reshape(b, s, n, HEAD_DIM).transpose(0, 2, 1, 3)

    y_a = _nsa(heads(q_a, NSA_HEADS), heads(kc, NSA_KV_GROUPS), heads(vc, NSA_KV_GROUPS),
               heads(ksl, NSA_KV_GROUPS), heads(vsl, NSA_KV_GROUPS), heads(kwn, NSA_KV_GROUPS),
               heads(vwn, NSA_KV_GROUPS), g_nsa, ck_pos, ck_w1, ck_w2, cv_pos, cv_w1, cv_w2) @ w_branch_a
    y_b = _dilated(_rope(heads(q_b, DIL_HEADS)), _rope(heads(k_b, DIL_HEADS)), heads(v_b, DIL_HEADS)) @ w_branch_b
    merged = jax.nn.sigmoid(g_a) * y_a + jax.nn.sigmoid(g_b) * y_b
    return merged @ w_o

def setup_inputs(seed: int = 0) -> dict:
    key = jax.random.key(seed)
    ks = jax.random.split(key, 26)
    L = DEPTH

    def nrm(k, shape, scale):
        return jax.random.normal(k, shape, jnp.float32) * scale

    def gain(k):
        return 1.0 + nrm(k, (L, D_MODEL), 0.02)

    return {
        "x": nrm(ks[0], (BATCH, SEQ, D_MODEL), 1.0),
        "ffn1_w_gate": nrm(ks[1], (L, D_MODEL, FFN_HIDDEN), D_MODEL ** -0.5),
        "ffn1_w_up": nrm(ks[2], (L, D_MODEL, FFN_HIDDEN), D_MODEL ** -0.5),
        "ffn1_w_down": nrm(ks[3], (L, FFN_HIDDEN, D_MODEL), DEEPNORM_BETA * FFN_HIDDEN ** -0.5),
        "ln_ffn1_g": gain(ks[4]),
        "ln_ffn1_b": nrm(ks[5], (L, D_MODEL), 0.02),
        "w_in": nrm(ks[6], (L, D_MODEL, IN_WIDTH), D_MODEL ** -0.5),
        "cmp_k_pos": nrm(ks[7], (L, CMP_BLOCK, HEAD_DIM), 0.1),
        "cmp_k_w1": nrm(ks[8], (L, CMP_BLOCK * HEAD_DIM, CMP_HIDDEN), (CMP_BLOCK * HEAD_DIM) ** -0.5),
        "cmp_k_w2": nrm(ks[9], (L, CMP_HIDDEN, HEAD_DIM), CMP_HIDDEN ** -0.5),
        "cmp_v_pos": nrm(ks[10], (L, CMP_BLOCK, HEAD_DIM), 0.1),
        "cmp_v_w1": nrm(ks[11], (L, CMP_BLOCK * HEAD_DIM, CMP_HIDDEN), (CMP_BLOCK * HEAD_DIM) ** -0.5),
        "cmp_v_w2": nrm(ks[12], (L, CMP_HIDDEN, HEAD_DIM), CMP_HIDDEN ** -0.5),
        "w_branch_a": nrm(ks[13], (L, BRANCH_A_W, D_MODEL), BRANCH_A_W ** -0.5),
        "w_branch_b": nrm(ks[14], (L, BRANCH_B_W, D_MODEL), BRANCH_B_W ** -0.5),
        "w_o": nrm(ks[15], (L, D_MODEL, D_MODEL), DEEPNORM_BETA * D_MODEL ** -0.5),
        "ln_mix_g": gain(ks[16]),
        "ln_mix_b": nrm(ks[17], (L, D_MODEL), 0.02),
        "ffn2_w_gate": nrm(ks[18], (L, D_MODEL, FFN_HIDDEN), D_MODEL ** -0.5),
        "ffn2_w_up": nrm(ks[19], (L, D_MODEL, FFN_HIDDEN), D_MODEL ** -0.5),
        "ffn2_w_down": nrm(ks[20], (L, FFN_HIDDEN, D_MODEL), DEEPNORM_BETA * FFN_HIDDEN ** -0.5),
        "ln_ffn2_g": gain(ks[21]),
        "ln_ffn2_b": nrm(ks[22], (L, D_MODEL), 0.02),
    }

def reference(x, ffn1_w_gate, ffn1_w_up, ffn1_w_down, ln_ffn1_g, ln_ffn1_b, w_in,
              cmp_k_pos, cmp_k_w1, cmp_k_w2, cmp_v_pos, cmp_v_w1, cmp_v_w2,
              w_branch_a, w_branch_b, w_o, ln_mix_g, ln_mix_b,
              ffn2_w_gate, ffn2_w_up, ffn2_w_down, ln_ffn2_g, ln_ffn2_b):
    h = x
    for l in range(DEPTH):
        h = _layer_norm(DEEPNORM_ALPHA * h + 0.5 * _swiglu(h, ffn1_w_gate[l], ffn1_w_up[l], ffn1_w_down[l]),
                        ln_ffn1_g[l], ln_ffn1_b[l])
        mix = _mixer(h, w_in[l], cmp_k_pos[l], cmp_k_w1[l], cmp_k_w2[l], cmp_v_pos[l], cmp_v_w1[l], cmp_v_w2[l],
                     w_branch_a[l], w_branch_b[l], w_o[l])
        h = _layer_norm(DEEPNORM_ALPHA * h + mix, ln_mix_g[l], ln_mix_b[l])
        h = _layer_norm(DEEPNORM_ALPHA * h + 0.5 * _swiglu(h, ffn2_w_gate[l], ffn2_w_up[l], ffn2_w_down[l]),
                        ln_ffn2_g[l], ln_ffn2_b[l])
    return h


_drawn_inputs = setup_inputs


def setup_inputs(seed=0):
    import zlib

    import numpy as np

    out = dict(_drawn_inputs(seed))
    spreads = {}
    factors = {'ln_ffn1_g': 2.817,
     'cmp_k_pos': 8.0,
     'cmp_k_w1': 3.51,
     'cmp_k_w2': 3.619,
     'cmp_v_pos': 7.875,
     'ln_mix_g': 2.877,
     'ln_mix_b': 2.799,
     'ln_ffn2_g': 7.648,
     'ln_ffn2_b': 7.817,
     'ln_ffn1_b': 4.314}
    for name, (base, spread) in spreads.items():
        noise = np.random.default_rng([zlib.crc32(name.encode()), seed]).standard_normal(out[name].shape)
        drawn = base * np.exp(spread * noise) if base else spread * noise
        out[name] = __import__('jax').numpy.asarray(drawn.astype(out[name].dtype))
    for name, factor in factors.items():
        out[name] = (out[name] * factor).astype(out[name].dtype)
    return out
```

```python
from contextlib import ExitStack

import numpy as np
import concourse.bass as bass
from concourse import mybir

F32 = mybir.dt.float32
F32R = mybir.dt.float32r
ALU = mybir.AluOpType
ACT = mybir.ActivationFunctionType
AX_X = mybir.AxisListType.X

P = 128
D = 2048
TOKENS = 256
TILES = TOKENS // P
HEAD = 128
HIDDEN = 5632
COLS = 512
KT = D // P
FT = HIDDEN // P
RING = 4
SLOT_KT = 2
SLOT = SLOT_KT * COLS
LAG = 2
BANKS = 4
ALPHA = 2.0 ** 0.25
EPS = 1e-5
SCALE = HEAD ** -0.5
MASKED = -1e30

GU_CHUNKS = HIDDEN // COLS
GU_SLOTS = KT // SLOT_KT
DOWN_SLOTS = FT // SLOT_KT
OUT_CHUNKS = D // COLS

GROUPS = 2
HPG = 4
NSA_HEADS = GROUPS * HPG
CMP_BLOCK, CMP_STRIDE = 32, 16
N_CMP = (TOKENS - CMP_BLOCK) // CMP_STRIDE + 1
CMP_HIDDEN = 2 * HEAD
CMP_SLOTS = CMP_BLOCK // 4
PATTERNS = ((128, 1), (512, 4), (2048, 16))
NSA_GATES = NSA_HEADS * 3
W_GATE0 = 2560
GELU_C = (2.0 / np.pi) ** 0.5

DIL0 = W_GATE0 + NSA_GATES
MIX_ORDER = [("kv", 1024), ("kv", 1536), ("kv", 2048), ("q", 0), ("q", 512), ("cmp", 0), ("cmp", 1)]
for _p in range(3):
    MIX_ORDER += [("q", DIL0 + _p * 512), ("k", DIL0 + 1536 + _p * 512), ("v", DIL0 + 3072 + _p * 512)]
MIX_ORDER += [("gate", DIL0 + 4608 + _n * 512) for _n in range(8)]
CHUNK_BUF = [0, 1, 2, 3, 4, None, None, 5, 6, 7, 8, 9, 10, 11, 12, 13, 0, 1, 2, 5, 6, 7, 3, 4]
MIX_SLOTS = 8 * len(MIX_ORDER)
SLC, WINDOW, CMP, DIL = range(4)
UNITS = [(SLC, 0, 44), (WINDOW, 0, 0), (SLC, 1, 0), (WINDOW, 1, 0), (CMP, 0, 0), (CMP, 1, 0),
         (DIL, 0, 86), (DIL, 1, 106), (DIL, 2, 131)]


class Plan:

    def __init__(self):
        self.k, self.uses, self.t, self.at, self.by_pos = 0, [0] * BANKS, {}, {}, {}


class Task:

    def __init__(self, k, bank_, use):
        self.k, self.bank, self.use = k, bank_, use


def plan():
    pl = Plan()

    def task(name, bank=None):
        b = pl.k % BANKS if bank is None else bank
        pl.t[name] = Task(pl.k, b, pl.uses[b])
        pl.k += 1
        pl.uses[b] += 1

    def ffn(f):
        for j in range(GU_SLOTS):
            task(("x", f, j), j % BANKS)
        if f == 0:
            task(("setup",), 2)
        for i in range(GU_CHUNKS):
            for half in range(2):
                task(("h", f, i, half), half)

    ffn(0)
    for j in range(GU_SLOTS):
        task(("x", "mix", j), j % BANKS)

    busy = set()

    def place(name, earliest):
        pos = earliest
        while pos in busy:
            pos += 1
        busy.add(pos)
        pl.at[name] = pos
        return pos

    place(("kcT",), 10)
    place(("vcT",), 11)
    place(("gates",), 36)
    place(("kcmp",), 62)
    place(("vcmp",), 63)
    scored = probs_read = pv_read = 0
    for u, (kind, g, ready) in enumerate(UNITS):
        first = max(ready, scored + 1)
        last = first
        if kind != WINDOW:
            for tile in range(TILES):
                last = place(("qT", u, tile), max(first, last))
        if kind == DIL or (kind == SLC and g == 0):
            for tile in range(TILES):
                last = place(("kT", u, tile), last)
        n_scores = 1 if kind == CMP else 3
        earliest = max(last + 5 if kind != WINDOW else scored + 1, probs_read - 1)
        for j in range(n_scores):
            earliest = place(("s", u, j), earliest)
        scored = earliest
        n_probs = 2 if kind == CMP else 3
        earliest = max(scored + 8, pv_read - 1)
        for j in range(n_probs):
            earliest = place(("pT", u, j), earliest)
        probs_read = earliest
        earliest += 5
        for tile in range(TILES):
            earliest = place(("pv", u, tile), earliest)
        pv_read = earliest
    for j in range(4):
        place(("oT", j), pv_read + 3)
    for j in range(2):
        place(("oT", 4 + j), pv_read + 11)
    assert max(busy) < MIX_SLOTS, max(busy)
    for name in sorted(pl.at, key=pl.at.get):
        task(name)
    for name, pos in pl.at.items():
        pl.by_pos.setdefault(pos, []).append(name)
    for n in range(OUT_CHUNKS):
        for half in range(2):
            task(("m", n, half))
    ffn(1)
    return pl


def mixer_constants():
    inv = (np.float32(10000.0) ** (-np.arange(0, HEAD, 2, dtype=np.float32) / np.float32(HEAD))).astype(np.float32)
    ang = np.arange(TOKENS, dtype=np.float32)[:, None] * inv[None, :]
    cos, sin = np.cos(ang), np.sin(ang)
    rope = np.stack([np.concatenate([cos, cos], 1), np.concatenate([-sin, sin], 1)])
    rope = rope.reshape(2, TILES, P, HEAD).transpose(2, 0, 1, 3)
    t, k = np.arange(P)[:, None] + P, np.arange(TOKENS)[None, :]
    masks = []
    for win, dil in ((TOKENS, 1),) + PATTERNS:
        d = t - k
        masks.append((d >= 0) & (d <= win) & (d % dil == 0))
    masks = np.where(np.stack(masks, 1), 0.0, MASKED)
    tt = np.arange(TOKENS)
    seen = (np.arange(N_CMP) * CMP_STRIDE + CMP_BLOCK - 1)[None, :] <= tt[:, None]
    cmask = np.where(seen, 0.0, MASKED).reshape(TILES, P, N_CMP).transpose(1, 0, 2)
    any_seen = seen.any(1).astype(np.float32).reshape(TILES, P).T
    small = np.concatenate([cmask.reshape(P, -1), any_seen, np.eye(P)], 1)
    return (np.ascontiguousarray(rope, np.float32), np.ascontiguousarray(masks, np.float32),
            np.ascontiguousarray(small, np.float32))


def build(nc, x, w1_gate, w1_up, w1_down, ln1_g, ln1_b, w_in, ck_pos, ck_w1, ck_w2, cv_pos, cv_w1, cv_w2,
          w_a, w_b, w_o, ln2_g, ln2_b, w2_gate, w2_up, w2_down, ln3_g, ln3_b, rope_c, masks_c, small_c, out):
    (w1_gate, w1_up, w1_down, ln1_g, ln1_b, w_in, ck_pos, ck_w1, ck_w2, cv_pos, cv_w1, cv_w2, w_a, w_b, w_o,
     ln2_g, ln2_b, w2_gate, w2_up, w2_down, ln3_g, ln3_b) = (
        a[0] for a in (w1_gate, w1_up, w1_down, ln1_g, ln1_b, w_in, ck_pos, ck_w1, ck_w2, cv_pos, cv_w1, cv_w2,
                       w_a, w_b, w_o, ln2_g, ln2_b, w2_gate, w2_up, w2_down, ln3_g, ln3_b))
    pl = plan()
    T = pl.t
    ctx = ExitStack()
    with ctx:
        def sb(name, shape, dt=F32, stack=ctx):
            return stack.enter_context(nc.sbuf_tensor(name, shape, dt))

        def sem(name):
            return ctx.enter_context(nc.semaphore(name))

        raw = sb("raw", [P, RING, SLOT])
        w_hi = sb("w_hi", [P, RING, SLOT], F32R)
        w_lo = sb("w_lo", [P, RING, SLOT], F32R)
        act_hi = sb("act_hi", [P, KT, TOKENS], F32R)
        act_lo = sb("act_lo", [P, KT, TOKENS], F32R)
        resid = sb("resid", [P, TILES, D])
        ln_nat = sb("ln_nat", [P, 2, D])
        over = ExitStack()
        cx = sb("cx", [P, 2, 4, 2, GROUPS * N_CMP], F32, over)
        kcmpT = sb("kcmpT", [P, GROUPS * N_CMP], F32, over)
        vcmp = sb("vcmp", [N_CMP, GROUPS, HEAD], F32, over)
        gates = sb("gates", [P, TILES, NSA_GATES], F32, over)
        coef = sb("coef", [P, 2, 8], F32, over)
        over.close()
        affine = sb("affine", [P, 2, 2, TOKENS])
        small = sb("small", [P, TILES * N_CMP + TILES + P])
        vec_rows = sb("vec_rows", [64, P])
        pos_rows = sb("pos_rows", [CMP_BLOCK, 2, P])
        vecT = sb("vecT", [P, 4 * KT + 2 * CMP_BLOCK])
        stats = sb("stats", [P, TILES, OUT_CHUNKS, 6])
        ln_s = sb("ln_s", [P, 8, TILES])
        mv = sb("mv", [P, TILES, 2])
        over = ExitStack()
        hT_hi = sb("hT_hi", [P, FT, TOKENS], F32R, over)
        hT_lo = sb("hT_lo", [P, FT, TOKENS], F32R, over)
        gate_t = sb("gate_t", [P, TILES, COLS], F32, over)
        hid = sb("hid", [P, TILES, COLS], F32, over)
        over.close()
        chunks_lo = sb("chunks_lo", [P, 8, TILES, COLS])
        over = ExitStack()
        oT_hi = sb("oT_hi", [P, 12, TOKENS], F32R, over)
        oT_lo = sb("oT_lo", [P, 12, TOKENS], F32R, over)
        over.close()
        over = ExitStack()
        kcvcT = sb("kcvcT", [P, 2, GROUPS, TOKENS], F32, over)
        blk = sb("blk", [P, CMP_BLOCK, GROUPS, N_CMP], F32, over)
        blk_hi = sb("blk_hi", [P, 2, CMP_BLOCK, GROUPS * N_CMP], F32R, over)
        blk_lo = sb("blk_lo", [P, 2, CMP_BLOCK, GROUPS * N_CMP], F32R, over)
        over.close()
        chunks_hi = sb("chunks_hi", [P, 6, TILES, COLS])
        rot_q = sb("rot_q", [P, TILES, COLS])
        rot_k = sb("rot_k", [P, TILES, COLS])
        rot_tmp = sb("rot_tmp", [P, TILES, COLS])
        qT = sb("qT", [P, HPG, TOKENS])
        kT = sb("kT", [P, HPG, TOKENS])
        over = ExitStack()
        wg_hi = sb("wg_hi", [P, KT, NSA_GATES], F32R, over)
        wg_lo = sb("wg_lo", [P, KT, NSA_GATES], F32R, over)
        over.close()
        s0 = sb("s0", [P, HPG, P])
        s1 = sb("s1", [P, HPG, TOKENS])
        pT = sb("pT", [P, 3, HPG, P])
        o_a = sb("o_a", [P, TILES, NSA_HEADS * HEAD])
        rope = sb("rope", [P, 2, TILES, HEAD])
        masks = sb("masks", [P, 4, TOKENS])
        wg_raw = o_a[:, 0, 0:KT * NSA_GATES].rearrange("p (t n) -> p t n", n=NSA_GATES)
        negmax = sb("negmax", [P, len(UNITS), 8])
        sums = sb("sums", [P, len(UNITS), 8])
        dilw = sb("dilw", [P, 6, 3, 8])

        def chunk_buf(order):
            b = CHUNK_BUF[order]
            return chunks_lo[:, b] if b < 8 else chunks_hi[:, b - 8]

        o_dil = [ln_nat[:, 0, 0:1024], ln_nat[:, 0, 1024:2048], ln_nat[:, 1, 0:1024]]
        o_dil = [v.rearrange("p (t n) -> p t n", t=TILES) for v in o_dil]
        o_b = ln_nat[:, 1, 1024:2048].rearrange("p (t n) -> p t n", t=TILES)
        o_add = ln_nat[:, 1, 1024:1536].rearrange("p (h n) -> p h n", h=HPG)
        cw2 = ln_nat[:, 1, 1536:2048].rearrange("p (v k n) -> p v k n", v=2, k=2)
        cmp_mask = small[:, 0:TILES * N_CMP].rearrange("p (t n) -> p t n", t=TILES)
        any_seen = small[:, TILES * N_CMP:TILES * N_CMP + TILES]
        ident = small[:, TILES * N_CMP + TILES:]
        posT = vecT[:, 4 * KT:].rearrange("p (v j) -> p v j", v=2)

        acc = ctx.enter_context(nc.psum_tensor("acc", [P, 4, 512], F32))
        bank = ctx.enter_context(nc.psum_tensor("bank", [P, BANKS, 512], F32))

        raw_loaded = [sem(f"raw_loaded{r}") for r in range(RING)]
        hi_done = sem("hi_done")
        lo_done = sem("lo_done")
        slots_used = sem("slots_used")
        acc_emptied = [sem("acc_emptied0"), sem("acc_emptied1")]
        bank_filled = sem("bank_filled")
        bank_emptied = [sem(f"bank_emptied{b}") for b in range(BANKS)]
        hi_moved = sem("hi_moved")
        x_loaded = [sem("x_loaded0"), sem("x_loaded1")]
        small_loaded = sem("small_loaded")
        consts_loaded = sem("consts_loaded")
        mix_consts_loaded = sem("mix_consts_loaded")
        cw2_loaded = sem("cw2_loaded")
        ln_nat_loaded = sem("ln_nat_loaded")
        resid_ready = sem("resid_ready")
        gate_tanh = sem("gate_tanh")
        var_ready = sem("var_ready")
        std_ready = sem("std_ready")
        norm_ready = sem("norm_ready")
        z_dve = sem("z_dve")
        z_act = sem("z_act")
        lo_pairs = sem("lo_pairs")
        stats_done = sem("stats_done")
        roped = sem("roped")
        blk_ready = sem("blk_ready")
        blk_rounded = sem("blk_rounded")
        blk_split = sem("blk_split")
        gelu_in = sem("gelu_in")
        gelu_tanh = sem("gelu_tanh")
        gelu_out = sem("gelu_out")
        wg_rounded = sem("wg_rounded")
        wg_split = sem("wg_split")
        gates_tanh = sem("gates_tanh")
        gates_ready = sem("gates_ready")
        max_ready = sem("max_ready")
        probs_ready = sem("probs_ready")
        o_ready = sem("o_ready")
        dil_shift = sem("dil_shift")
        dil_exp = sem("dil_exp")
        ob_ready = sem("ob_ready")
        merged = sem("merged")
        dve_step = sem("dve_step")
        pool_step = sem("pool_step")
        out_ready = sem("out_ready")
        out_ready_pool = sem("out_ready_pool")
        stored = sem("stored")

        gu_slot = [0, 0]
        down_slot = [GU_CHUNKS * 2 * GU_SLOTS, 0]
        mix_slot = down_slot[0] + OUT_CHUNKS * DOWN_SLOTS
        tail_slot = mix_slot + MIX_SLOTS
        TAIL_SLOTS = OUT_CHUNKS * 6 + OUT_CHUNKS * GU_SLOTS
        gu_slot[1] = tail_slot + TAIL_SLOTS
        down_slot[1] = gu_slot[1] + GU_CHUNKS * 2 * GU_SLOTS
        gu_acc = [0, 0]
        down_acc = [2 * GU_CHUNKS, 0]
        mix_acc = down_acc[0] + OUT_CHUNKS
        ab_acc = mix_acc + len(MIX_ORDER)
        o_acc = ab_acc + 2 * OUT_CHUNKS
        gu_acc[1] = o_acc + OUT_CHUNKS
        down_acc[1] = gu_acc[1] + 2 * GU_CHUNKS
        assert all(v % 4 == 0 for v in (*gu_slot, *down_slot, mix_slot, tail_slot))
        assert all(v % 2 == 0 for v in (*gu_acc, *down_acc, mix_acc, ab_acc, o_acc))

        def ring_turn(n0, i, per, s):
            return i * (per // RING) + (n0 + s) // RING + 1

        def load_slot(sp, src, n0, i, per, s):
            if not (isinstance(i, int) and n0 + i * per + s < RING):
                sp.wait_ge(lo_done, i * per + (n0 + s - RING + 1))
            r = (n0 + s) % RING
            dst = raw[:, r, :].rearrange("p (t n) -> p t n", n=src.shape[2])
            sp.dma_start(dst, src).then_inc(raw_loaded[r], 16)

        def round_slot(act, n0, i, per, s):
            r = (n0 + s) % RING
            act.wait_ge(raw_loaded[r], ring_turn(n0, i, per, s) * 16)
            if not (isinstance(i, int) and n0 + i * per + s < RING):
                act.wait_ge(slots_used, i * per + (n0 + s - RING + 1))
            nc.scalar.activation(w_hi[:, r, :], raw[:, r, :], ACT.Copy).then_inc(hi_done, 1)

        def split_slot(dve, n0, i, per, s):
            r = (n0 + s) % RING
            dve.wait_ge(hi_done, i * per + (n0 + s + 1))
            nc.vector.tensor_tensor(w_lo[:, r, :], raw[:, r, :], w_hi[:, r, :].bitcast(F32),
                                    ALU.subtract).then_inc(lo_done, 1)

        def multiply_slot(pe, a_hi, a_lo, kt0, pair, first, last, n0, i, per, s):
            r = (n0 + s) % RING
            pe.wait_ge(lo_done, i * per + (n0 + s + 1))
            for k in range(SLOT_KT):
                hi = w_hi[:, r, k * COLS:(k + 1) * COLS]
                lo = w_lo[:, r, k * COLS:(k + 1) * COLS]
                for tile in range(TILES):
                    o = acc[:, 2 * pair + tile, :]
                    ah = a_hi[:, kt0 + k, tile * P:(tile + 1) * P]
                    al = a_lo[:, kt0 + k, tile * P:(tile + 1) * P]
                    nc.tensor.matmul(o, ah, hi, start=first and k == 0, stop=False)
                    nc.tensor.matmul(o, ah, lo, start=False, stop=False)
                    mm = nc.tensor.matmul(o, al, hi, start=False, stop=last and k == SLOT_KT - 1)
            mm.then_inc(slots_used, 1)

        def wait_acc_full(eng, slot_end):
            eng.wait_ge(slots_used, slot_end)

        def wait_acc_free(pe, c0, i, per, c):
            if not (isinstance(i, int) and c0 + i * per + c < 2):
                pe.wait_ge(acc_emptied[(c0 + c) % 2], i * (per // 2) + (c0 + c) // 2)

        def acc_pair(c):
            return acc[:, 2 * (c % 2):2 * (c % 2) + 2, :]

        def wait_filled(eng, t):
            eng.wait_ge(bank_filled, t.k + 1)

        def wait_bank_free(pe, t):
            if t.use:
                pe.wait_ge(bank_emptied[t.bank], t.use)

        def wait_moved(eng, t):
            eng.wait_ge(bank_emptied[t.bank], t.use + 1)

        def transpose_pair(src, col, b):
            for k in range(2):
                for tile in range(TILES):
                    mm = nc.tensor.transpose(bank[:, b, k * TOKENS + tile * P:k * TOKENS + (tile + 1) * P],
                                             src[:, tile, col + k * P:col + (k + 1) * P], ident)
            mm.then_inc(bank_filled, 1)

        moved = {}
        n_hi = 0
        hi_order = [("x", 0, j) for j in range(8)]
        hi_order += [("h", 0, i, half) for i in range(GU_CHUNKS) for half in range(2)]
        hi_order += [("x", "mix", j) for j in range(8)]
        hi_order += [("oT", j) for j in range(6)]
        hi_order += [("m", n, half) for n in range(OUT_CHUNKS) for half in range(2)]
        hi_order += [("x", 1, j) for j in range(8)]
        hi_order += [("h", 1, i, half) for i in range(GU_CHUNKS) for half in range(2)]
        for name in hi_order:
            moved[name] = n_hi
            n_hi += 1

        def pair_of(t_, kt):
            return t_[:, kt:kt + 2, :].rearrange("p k n -> p (k n)")

        def round_pair(act, name, dst, scale=1.0):
            t = T[name]
            wait_filled(act, t)
            nc.scalar.activation(dst, bank[:, t.bank, :], ACT.Copy, scale=scale).then_inc(hi_moved, 1)

        def split_pair(dve, name, dst, hi, scale=1.0):
            t = T[name]
            dve.wait_ge(hi_moved, moved[name] + 1)
            nc.vector.scalar_tensor_tensor(dst, bank[:, t.bank, :], scale, hi.bitcast(F32), ALU.mult,
                                           ALU.subtract).then_inc(bank_emptied[t.bank], 1)

        w_gu = [(w1_gate, w1_up), (w2_gate, w2_up)]
        w_dn = [w1_down, w2_down]

        def rows(w):
            return w.rearrange("(t p) n -> p t n", p=P)

        def bank_use(name, i):
            return i + T[name].use

        mix_src = []
        for kind, col in MIX_ORDER:
            for s in range(8):
                if kind == "cmp":
                    w = (ck_w1, cv_w1)[col]
                    mix_src.append(rows(w)[:, 4 * s:4 * s + 4, :])
                else:
                    mix_src.append(rows(w_in)[:, 2 * s:2 * s + 2, col:col + COLS])
        for n in range(OUT_CHUNKS):
            for w, ns in ((w_a, 4), (w_b, 2)):
                mix_src += [rows(w)[:, 2 * s:2 * s + 2, n * COLS:(n + 1) * COLS] for s in range(ns)]
        for n in range(OUT_CHUNKS):
            mix_src += [rows(w_o)[:, 2 * s:2 * s + 2, n * COLS:(n + 1) * COLS] for s in range(8)]
        assert len(mix_src) == MIX_SLOTS + TAIL_SLOTS

        merge_at = {6 * n + 5 + 3: n for n in range(OUT_CHUNKS)}

        def gate_chunk(act, order):
            wait_acc_full(act, mix_slot + 8 * (order + 1))
            b = CHUNK_BUF[order]
            last = ("pv", 3, 1) if b < 3 else ("pv", 6, 1) if b >= 5 else ("qT", 5, 1)
            wait_filled(act, T[last])
            nc.scalar.activation(chunk_buf(order), acc_pair(mix_acc + order), ACT.Tanh, scale=0.5) \
                .then_inc(acc_emptied[(mix_acc + order) % 2], 1)

        def move_heads(act, name, t):
            u = name[1]
            wait_filled(act, t)
            src = bank[:, t.bank, :].rearrange("p (h n) -> p h n", n=P)
            dst = qT if name[0] == "qT" else kT
            nc.scalar.activation(dst[:, :, name[2] * P:(name[2] + 1) * P], src, ACT.Copy) \
                .then_inc(bank_emptied[t.bank], 1)

        n_exps = [1 if kind == CMP else 2 * HPG for kind, _, _ in UNITS]
        exps_before = [sum(n_exps[:u]) for u in range(len(UNITS) + 1)]

        def exponentials(act, u):
            kind = UNITS[u][0]
            act.wait_ge(max_ready, u + 1)
            if kind == CMP:
                v = s0[:, 0, 0:8 * N_CMP]
                nc.scalar.activation(v, v, ACT.Exp, scale=SCALE).then_inc(probs_ready, 1)
                return
            for e in range(2 * HPG):
                v = s0[:, e] if e < HPG else s1[:, e - HPG]
                nc.scalar.activation(v, v, ACT.Exp, bias=negmax[:, u, e:e + 1], scale=SCALE,
                                     accum_out=sums[:, u, e:e + 1]).then_inc(probs_ready, 1)

        block = ctx.enter_context(nc.Block())

        @block.sync
        def _(sp):
            for tile in range(TILES):
                sp.dma_start(resid[:, tile, :], x[0].rearrange("(t p) d -> p t d", p=P)[:, tile, :]) \
                    .then_inc(x_loaded[tile], 16)
                if tile == 0:
                    sp.dma_start(small[:, :], small_c).then_inc(small_loaded, 16)

            def gu_chunk(f, i):
                for h in range(2):
                    for s in range(GU_SLOTS):
                        src = rows(w_gu[f][h])[:, 2 * s:2 * s + 2, bass.ds(i * COLS, COLS)]
                        load_slot(sp, src, gu_slot[f], i, 2 * GU_SLOTS, h * GU_SLOTS + s)

            def ffn(f):
                gu_chunk(f, 0)
                if f == 0:
                    for v, a in enumerate((ln1_g, ln1_b, ln2_g, ln2_b)):
                        sp.dma_start(vec_rows[16 * v:16 * v + 16, :], a.rearrange("(t p) -> t p", p=P)) \
                            .then_inc(consts_loaded, 16)
                    sp.dma_start(pos_rows[:, 0, :], ck_pos).then_inc(consts_loaded, 16)
                    sp.dma_start(pos_rows[:, 1, :], cv_pos).then_inc(consts_loaded, 16)
                    load_ln(0)
                with sp.Fori(1, GU_CHUNKS) as i:
                    gu_chunk(f, i)
                if f == 1:
                    sp.wait_ge(resid_ready, 3)
                    load_ln(2)
                with sp.Fori(0, 2) as i:
                    for c in range(2):
                        for s in range(DOWN_SLOTS):
                            src = rows(w_dn[f])[:, 2 * s:2 * s + 2, bass.ds(i * (2 * COLS) + c * COLS, COLS)]
                            load_slot(sp, src, down_slot[f], i, 2 * DOWN_SLOTS, c * DOWN_SLOTS + s)

            def load_ln(which):
                g, b = ((ln1_g, ln1_b), (ln2_g, ln2_b), (ln3_g, ln3_b))[which]
                for v, a in enumerate((g, b)):
                    sp.dma_start(ln_nat[:, v, :], a.rearrange("(a n) -> a n", a=1).broadcast_to([P, D])) \
                        .then_inc(ln_nat_loaded, 16)

            ffn(0)
            for pos in range(MIX_SLOTS + TAIL_SLOTS):
                load_slot(sp, mix_src[pos], mix_slot, 0, 0, pos)
                if pos == 4:
                    sp.wait_ge(slots_used, mix_slot)
                    sp.dma_start(rope[:, :, :, :], rope_c).then_inc(mix_consts_loaded, 16)
                    sp.dma_start(masks[:, :, :], masks_c).then_inc(mix_consts_loaded, 16)
                    sp.dma_start(wg_raw, rows(w_in)[:, :, W_GATE0:W_GATE0 + NSA_GATES]) \
                        .then_inc(mix_consts_loaded, 16)
                if pos == 32:
                    sp.wait_ge(resid_ready, 2)
                    for v, w in enumerate((ck_w2, cv_w2)):
                        sp.dma_start(cw2[:, v, :, :], w.rearrange("(t p) n -> p t n", p=P)) \
                            .then_inc(cw2_loaded, 16)
                if pos == MIX_SLOTS + 8:
                    wait_filled(sp, T[("oT", 5)])
                    load_ln(1)

            ffn(1)
            out_t = out[0].rearrange("(t p) d -> p t d", p=P)
            for tile, ready in ((0, out_ready), (1, out_ready_pool)):
                sp.wait_ge(ready, 1)
                sp.dma_start(out_t[:, tile, :], resid[:, tile, :]).then_inc(stored, 16)
            sp.wait_ge(stored, 16 * TILES)

        @block.scalar
        def _(act):
            def gu_chunk(f, i, peel):
                per, c0 = 2 * GU_SLOTS, gu_acc[f]
                for s in range(2 * GU_SLOTS):
                    if not (peel and s < 3):
                        round_slot(act, gu_slot[f], i, per, s)
                    if peel and s >= 2 and s - 2 < 8:
                        x_pairs(f, s - 2)
                    if s == GU_SLOTS - 1 + LAG:
                        act.wait_ge(slots_used, i * per + (gu_slot[f] + GU_SLOTS))
                        if not (peel and f == 0):
                            act.wait_ge(acc_emptied[1], i + (c0 // 2))
                        nc.scalar.activation(gate_t[:, :, :], acc_pair(0), ACT.Tanh, scale=0.5).then_inc(gate_tanh, 1)
                    if not peel and s in (5, 6):
                        round_h(f, i, s - 5)

            def round_h(f, i, half):
                t = T[("h", f, 0, half)]
                act.wait_ge(bank_filled, i * 2 + (t.k + 1 - 2))
                dst = hT_hi[:, bass.ds(i * 4 + (2 * half - 4), 2), :] if not isinstance(i, int) else \
                    hT_hi[:, i * 4 + 2 * half - 4:i * 4 + 2 * half - 2, :]
                nc.scalar.activation(dst, bank[:, half, :].rearrange("p (k n) -> p k n", k=2), ACT.Copy).then_inc(hi_moved, 1)

            def x_pairs(f, j):
                if f == 0:
                    round_pair(act, ("x", 0, j), pair_of(act_hi, 2 * j))
                else:
                    wait_moved(act, T[("x", f, j)])
                    nc.scalar.activation(pair_of(act_hi, 2 * j), affine[:, j % 2].rearrange("p k n -> p (k n)"),
                                         ACT.Copy).then_inc(hi_moved, 1)

            def down(f):
                with act.Fori(0, 2) as i:
                    for s in range(2 * DOWN_SLOTS):
                        round_slot(act, down_slot[f], i, 2 * DOWN_SLOTS, s)

            def layer_norm_act(which):
                act.wait_ge(var_ready, which + 1)
                nc.scalar.activation(ln_s[:, 1, :], ln_s[:, 0, :], ACT.Sqrt).then_inc(std_ready, 1)
                act.wait_ge(norm_ready, which + 1)
                for half in range(2):
                    v = resid[:, 1, half * 1024:(half + 1) * 1024]
                    nc.scalar.activation(v, v, ACT.Identity, bias=ln_s[:, 4, 1:2], scale=ln_s[:, 3, 1:2]).then_inc(z_act, 1)

            for s in range(3):
                round_slot(act, gu_slot[0], 0, 0, s)
            gu_chunk(0, 0, True)
            with act.Fori(1, GU_CHUNKS) as i:
                gu_chunk(0, i, False)
            for half in range(2):
                round_h(0, GU_CHUNKS, half)
            down(0)

            exp_at, dil_at = {}, None
            for u, (kind, g, _) in enumerate(UNITS):
                exp_at[pl.at[("s", u, 0 if kind == CMP else 2)] + LAG + 1] = u
            for s in range(3):
                round_slot(act, mix_slot, 0, 0, s)
            layer_norm_act(0)
            for pos in range(MIX_SLOTS):
                if pos >= 3:
                    round_slot(act, mix_slot, 0, 0, pos)
                if 2 <= pos < 10:
                    x_pairs("mix", pos - 2)
                if pos == 20:
                    act.wait_ge(mix_consts_loaded, 48)
                    nc.scalar.activation(wg_hi[:, :, :], wg_raw, ACT.Copy).then_inc(wg_rounded, 1)
                if pos in (24, 30):
                    v = (pos - 24) // 6
                    act.wait_ge(blk_ready, v + 1)
                    nc.scalar.activation(blk_hi[:, v], blk[:, :, :, :].rearrange("p j g n -> p j (g n)"),
                                         ACT.Copy).then_inc(blk_rounded, 1)
                order, end = divmod(pos - LAG, 8)
                if end == 7 and order >= 0:
                    kind, col = MIX_ORDER[order]
                    if kind == "cmp":
                        act.wait_ge(gelu_in, col + 1)
                        nc.scalar.activation(cx[:, col, 2], cx[:, col, 1], ACT.Tanh, scale=GELU_C).then_inc(gelu_tanh, 1)
                    if kind == "gate":
                        gate_chunk(act, order)
                for name in pl.by_pos.get(pos - LAG, ()):
                    t = T[name]
                    if name[0] in ("kcT", "vcT"):
                        wait_filled(act, t)
                        nc.scalar.activation(kcvcT[:, int(name[0] == "vcT")].rearrange("p g n -> p (g n)"),
                                             bank[:, t.bank, :], ACT.Copy).then_inc(bank_emptied[t.bank], 1)
                    elif name[0] == "gates":
                        wait_filled(act, t)
                        nc.scalar.activation(gates[:, :, :], bank[:, t.bank, 0:TILES * NSA_GATES]
                                             .rearrange("p (t n) -> p t n", t=TILES), ACT.Tanh, scale=0.5) \
                            .then_inc(bank_emptied[t.bank], 1)
                    elif name[0] == "kcmp":
                        wait_filled(act, t)
                        nc.scalar.activation(kcmpT[:, :], bank[:, t.bank, 0:GROUPS * N_CMP], ACT.Copy, scale=0.5) \
                            .then_inc(bank_emptied[t.bank], 1)
                    elif name[0] == "vcmp":
                        wait_filled(act, t)
                        nc.scalar.activation(vcmp[:, :, :], bank[0:N_CMP, t.bank, 0:GROUPS * HEAD]
                                             .rearrange("p (g n) -> p g n", g=GROUPS), ACT.Copy, scale=0.5) \
                            .then_inc(bank_emptied[t.bank], 1)
                    elif name[0] in ("qT", "kT"):
                        move_heads(act, name, t)
                    elif name[0] == "pv" and UNITS[name[1]][0] == DIL:
                        wait_filled(act, t)
                        p_ = UNITS[name[1]][1]
                        act.wait_ge(resid_ready, 2)
                        nc.scalar.activation(o_dil[p_][:, name[2], :], bank[:, t.bank, :], ACT.Copy) \
                            .then_inc(bank_emptied[t.bank], 1)
                    elif name[0] == "oT":
                        round_pair(act, name, pair_of(oT_hi, 2 * name[1]))
                if pos in exp_at:
                    exponentials(act, exp_at[pos])
                if pos == pl.at[("pv", len(UNITS) - 1, 1)] + LAG + 2:
                    act.wait_ge(dil_shift, 1)
                    nc.scalar.activation(dilw[:, 1], dilw[:, 0], ACT.Exp).then_inc(dil_exp, 1)

            for pos in range(TAIL_SLOTS):
                round_slot(act, tail_slot, 0, 0, pos)
                if pos == LAG - 1:
                    gate_chunk(act, len(MIX_ORDER) - 1)
                for d in range(2):
                    if pos - LAG - d in merge_at:
                        n = merge_at[pos - LAG - d]
                        round_pair(act, ("m", n, d), pair_of(act_hi, 4 * n + 2 * d), 0.5)

            for s in range(3):
                round_slot(act, gu_slot[1], 0, 0, s)
            layer_norm_act(1)
            gu_chunk(1, 0, True)
            with act.Fori(1, GU_CHUNKS) as i:
                gu_chunk(1, i, False)
            for half in range(2):
                round_h(1, GU_CHUNKS, half)
            down(1)
            layer_norm_act(2)

        @block.vector
        def _(dve):
            steps = [0]

            def link(ins):
                steps[0] += 1
                ins.then_inc(dve_step, 1)
                dve.wait_ge(dve_step, steps[0])

            def gu_chunk(f, i, peel):
                per = 2 * GU_SLOTS
                for s in range(2 * GU_SLOTS):
                    if not (peel and s < 3):
                        split_slot(dve, gu_slot[f], i, per, s)
                    if peel and s >= 2 and s - 2 < 8:
                        x_pairs(f, s - 2)
                    if f == 0 and peel and s == 11:
                        t = T[("setup",)]
                        wait_filled(dve, t)
                        nc.vector.tensor_copy(vecT[:, :], bank[:, t.bank, 0:128]).then_inc(bank_emptied[t.bank], 1)
                    if not peel and s == 1:
                        up_half(f, i)
                    if not peel and s in (5, 6):
                        split_h(f, i, s - 5)
                    if s == GU_SLOTS - 1 + LAG:
                        dve.wait_ge(gate_tanh, i + (GU_CHUNKS * f + 1))
                        nc.vector.scalar_tensor_tensor(gate_t[:, :, :], gate_t[:, :, :], 1.0, acc_pair(0), ALU.add,
                                                       ALU.mult).then_inc(acc_emptied[0], 1)

            def up_half(f, i):
                per, c0 = 2 * GU_SLOTS, gu_acc[f]
                dve.wait_ge(slots_used, i * per + gu_slot[f])
                dve.wait_ge(acc_emptied[0], i + (c0 // 2))
                if not (isinstance(i, int) and i == 1):
                    dve.wait_ge(bank_filled, i * 2 + (T[("h", f, 0, 0)].k - 2))
                nc.vector.tensor_tensor(hid[:, :, :], gate_t[:, :, :], acc_pair(1), ALU.mult).then_inc(acc_emptied[1], 1)

            def split_h(f, i, half):
                dve.wait_ge(hi_moved, i * 2 + (moved[("h", f, 0, half)] + 1 - 2))
                if isinstance(i, int):
                    k0 = slice(i * 4 + 2 * half - 4, i * 4 + 2 * half - 2)
                else:
                    k0 = bass.ds(i * 4 + (2 * half - 4), 2)
                nc.vector.tensor_tensor(hT_lo[:, k0, :], bank[:, half, :].rearrange("p (k n) -> p k n", k=2),
                                        hT_hi[:, k0, :].bitcast(F32), ALU.subtract).then_inc(bank_emptied[half], 1)

            def x_pairs(f, j):
                if f == 0:
                    split_pair(dve, ("x", 0, j), pair_of(act_lo, 2 * j), pair_of(act_hi, 2 * j))
                    return
                name = ("x", f, j)
                t = T[name]
                ln = 1 if f == 1 else 0
                if j == 0:
                    affine_pair(ln, t, j)
                if j + 1 < GU_SLOTS:
                    affine_pair(ln, T[("x", f, j + 1)], j + 1)
                dve.wait_ge(hi_moved, moved[name] + 1)
                nc.vector.tensor_tensor(pair_of(act_lo, 2 * j), affine[:, j % 2].rearrange("p k n -> p (k n)"),
                                        pair_of(act_hi, 2 * j).bitcast(F32), ALU.subtract).then_inc(lo_pairs, 1)
                dve.wait_ge(lo_pairs, 8 * ln + j + 1)

            def affine_pair(ln, t, j):
                wait_filled(dve, t)
                for k in range(2):
                    g = vecT[:, 32 * ln + 2 * j + k:32 * ln + 2 * j + k + 1]
                    b = vecT[:, 32 * ln + 16 + 2 * j + k:32 * ln + 16 + 2 * j + k + 1]
                    ins = nc.vector.tensor_scalar(affine[:, j % 2, k], bank[:, t.bank, k * TOKENS:(k + 1) * TOKENS],
                                                  g, b, ALU.mult, ALU.add)
                    if k == 0:
                        link(ins)
                ins.then_inc(bank_emptied[t.bank], 1)
                wait_moved(dve, t)

            def add_chunk(f, i, c, scale, n_slots, slot0, acc0):
                col = i * (2 * COLS) + c * COLS
                cs = slice(col, col + COLS) if isinstance(i, int) else bass.ds(col, COLS)
                pair = (acc0 + c) % 2
                dve.wait_ge(slots_used, i * (2 * n_slots) + (slot0 + (c + 1) * n_slots))
                nc.vector.scalar_tensor_tensor(resid[:, :, cs], acc_pair(pair), scale, resid[:, :, cs], ALU.mult,
                                               ALU.add).then_inc(acc_emptied[pair], 1)
                dve.wait_ge(acc_emptied[pair], i + ((acc0 + c) // 2 + 1))
                for tile in range(TILES):
                    nc.vector.bn_stats(stats[:, tile, bass.ds(i * 2 + c, 1), :].rearrange("p a b -> p (a b)")
                                       if not isinstance(i, int) else stats[:, tile, i * 2 + c, :],
                                       resid[:, tile, cs]).then_inc(stats_done, 1)

            def add_chunk_static(c):
                add_chunk(None, 0, c, 1.0, 8, tail_slot + 6 * OUT_CHUNKS, o_acc)

            def down(f):
                dve.wait_ge(resid_ready, 1 if f == 0 else 3)
                with dve.Fori(0, 2) as i:
                    for c in range(2):
                        for s in range(DOWN_SLOTS):
                            split_slot(dve, down_slot[f], i, 2 * DOWN_SLOTS, c * DOWN_SLOTS + s)
                            if c == 1 and s == LAG:
                                add_chunk(f, i, 0, 0.25, DOWN_SLOTS, down_slot[f], down_acc[f])
                    add_chunk(f, i, 1, 0.25, DOWN_SLOTS, down_slot[f], down_acc[f])

            def layer_norm(which):
                dve.wait_ge(stats_done, 8 * (which + 1))
                for tile in range(TILES):
                    link(nc.vector.bn_aggr(mv[:, tile, :], stats[:, tile, :, :]))
                nc.vector.tensor_scalar(ln_s[:, 0, :], mv[:, :, 1], EPS, None, ALU.add).then_inc(var_ready, 1)
                dve.wait_ge(std_ready, which + 1)
                link(nc.vector.reciprocal(ln_s[:, 2, :], ln_s[:, 1, :]))
                link(nc.vector.tensor_tensor(ln_s[:, 5, :], ln_s[:, 2, :], ln_s[:, 2, :], ALU.mult))
                link(nc.vector.tensor_tensor(ln_s[:, 5, :], ln_s[:, 5, :], ln_s[:, 0, :], ALU.mult))
                link(nc.vector.tensor_scalar(ln_s[:, 5, :], ln_s[:, 5, :], -0.5, 1.5, ALU.mult, ALU.add))
                link(nc.vector.tensor_tensor(ln_s[:, 3, :], ln_s[:, 2, :], ln_s[:, 5, :], ALU.mult))
                nc.vector.scalar_tensor_tensor(ln_s[:, 4, :], mv[:, :, 0], -1.0, ln_s[:, 3, :], ALU.mult,
                                               ALU.mult).then_inc(norm_ready, 1)
                dve.wait_ge(norm_ready, which + 1)
                for half in range(2):
                    v = resid[:, 0, half * 1024:(half + 1) * 1024]
                    nc.vector.tensor_scalar(v, v, ln_s[:, 3, 0:1], ln_s[:, 4, 0:1], ALU.mult, ALU.add).then_inc(z_dve, 1)

            for s in range(3):
                split_slot(dve, gu_slot[0], 0, 0, s)
            gu_chunk(0, 0, True)
            with dve.Fori(1, GU_CHUNKS) as i:
                gu_chunk(0, i, False)
            up_half(0, GU_CHUNKS)
            for half in range(2):
                split_h(0, GU_CHUNKS, half)
            down(0)

            for s in range(3):
                split_slot(dve, mix_slot, 0, 0, s)
            layer_norm(0)
            max_at = {}
            for u, (kind, g, _) in enumerate(UNITS):
                max_at[pl.at[("s", u, 0 if kind == CMP else 2)] + LAG] = u
            unit_out = [0]

            def mask_scores(name, t):
                _, u, j = name
                kind, g, _ = UNITS[u]
                wait_filled(dve, t)
                if u:
                    last = max(T[("pT", u - 1, jj)].k for jj in range(2 if UNITS[u - 1][0] == CMP else 3))
                    dve.wait_ge(bank_filled, last + 1)
                m = 0 if kind != DIL else 1 + g
                if kind == CMP:
                    src = bank[:, t.bank, 0:8 * N_CMP].rearrange("p (t h n) -> p t h n", t=TILES, h=HPG)
                    dst = s0[:, 0, 0:8 * N_CMP].rearrange("p (t h n) -> p t h n", t=TILES, h=HPG)
                    msk = cmp_mask.unsqueeze(2).broadcast_to([P, TILES, HPG, N_CMP])
                elif j < 2:
                    src = bank[:, t.bank, :].rearrange("p (h n) -> p h n", h=2)
                    dst = s1[:, 2 * j:2 * j + 2, :]
                    msk = masks[:, m, :].unsqueeze(1).broadcast_to([P, 2, TOKENS])
                else:
                    src = bank[:, t.bank, :].rearrange("p (h n) -> p h n", h=HPG)
                    dst = s0[:, :, :]
                    msk = masks[:, m, P:TOKENS].unsqueeze(1).broadcast_to([P, HPG, P])
                nc.vector.tensor_tensor(dst, src, msk, ALU.add).then_inc(bank_emptied[t.bank], 1)

            def maxima(u):
                kind = UNITS[u][0]
                for j in range(1 if kind == CMP else 3):
                    wait_moved(dve, T[("s", u, j)])
                if kind == CMP:
                    v = s0[:, 0, 0:8 * N_CMP].rearrange("p (e n) -> p e n", e=8)
                    link(nc.vector.tensor_reduce(negmax[:, u, :], v, AX_X, ALU.max))
                    nc.vector.tensor_tensor(v, v, negmax[:, u, :].unsqueeze(2).broadcast_to([P, 8, N_CMP]),
                                            ALU.subtract).then_inc(max_ready, 1)
                    return
                link(nc.vector.tensor_reduce(negmax[:, u, 0:HPG], s0[:, :, :], AX_X, ALU.max))
                link(nc.vector.tensor_reduce(negmax[:, u, HPG:2 * HPG], s1[:, :, :], AX_X, ALU.max))
                nc.vector.tensor_scalar(negmax[:, u, :], negmax[:, u, :], -SCALE, None, ALU.mult).then_inc(max_ready, 1)

            def coefficients(u):
                kind, g, _ = UNITS[u]
                dve.wait_ge(probs_ready, exps_before[u + 1])
                link(nc.vector.reciprocal(coef[:, 0, :], sums[:, u, :]))
                branch = {CMP: 0, SLC: 1, WINDOW: 2}[kind]
                gv = gates[:, :, :].rearrange("p t (h b) -> p t h b", b=3)[:, :, HPG * g:HPG * g + HPG, branch]
                c = coef[:, 0, :].rearrange("p (t h) -> p t h", t=TILES)
                link(nc.vector.tensor_tensor(coef[:, 1, :].rearrange("p (t h) -> p t h", t=TILES), c, gv, ALU.mult))
                if kind == CMP:
                    c1 = coef[:, 1, :].rearrange("p (t h) -> p t h", t=TILES)
                    link(nc.vector.tensor_tensor(c1, c1, any_seen.unsqueeze(2).broadcast_to([P, TILES, HPG]), ALU.mult))

            def add_values(name, t):
                _, u, tile = name
                kind, g, _ = UNITS[u]
                if tile == 0:
                    coefficients(u)
                wait_filled(dve, t)
                src = bank[:, t.bank, :].rearrange("p (h n) -> p h n", h=HPG)
                dst = o_a[:, tile, g * 512:(g + 1) * 512].rearrange("p (h n) -> p h n", h=HPG)
                c = coef[:, 1, tile * HPG:(tile + 1) * HPG].unsqueeze(2).broadcast_to([P, HPG, HEAD])
                if kind == SLC:
                    nc.vector.tensor_tensor(dst, src, c, ALU.mult).then_inc(bank_emptied[t.bank], 1)
                    wait_moved(dve, t)
                else:
                    tmp = o_add[:, :, :]
                    nc.vector.tensor_tensor(tmp, src, c, ALU.mult).then_inc(bank_emptied[t.bank], 1)
                    wait_moved(dve, t)
                    unit_out[0] += 1
                    nc.vector.tensor_tensor(dst, dst, tmp, ALU.add).then_inc(o_ready, 1)
                    dve.wait_ge(o_ready, unit_out[0])

            def dilated_shift():
                d = [u for u, (kind, _, _) in enumerate(UNITS) if kind == DIL]
                dve.wait_ge(probs_ready, exps_before[-1])
                link(nc.vector.tensor_tensor(dilw[:, 2, 0], negmax[:, d[0], :], negmax[:, d[1], :], ALU.min))
                link(nc.vector.tensor_tensor(dilw[:, 2, 0], dilw[:, 2, 0], negmax[:, d[2], :], ALU.min))
                nc.vector.tensor_tensor(dilw[:, 0], dilw[:, 2, 0:1].broadcast_to([P, 3, 8]), negmax[:, d[0]:d[2] + 1, :],
                                        ALU.subtract).then_inc(dil_shift, 1)

            def dilated_merge():
                d = [u for u, (kind, _, _) in enumerate(UNITS) if kind == DIL]
                dve.wait_ge(dil_exp, 1)
                link(nc.vector.tensor_tensor(dilw[:, 3], dilw[:, 1], sums[:, d[0]:d[2] + 1, :], ALU.mult))
                link(nc.vector.tensor_tensor(dilw[:, 4, 0], dilw[:, 3, 0], dilw[:, 3, 1], ALU.add))
                link(nc.vector.tensor_tensor(dilw[:, 4, 0], dilw[:, 4, 0], dilw[:, 3, 2], ALU.add))
                link(nc.vector.reciprocal(dilw[:, 4, 1], dilw[:, 4, 0]))
                link(nc.vector.tensor_tensor(dilw[:, 5], dilw[:, 1], dilw[:, 4, 1:2].broadcast_to([P, 3, 8]), ALU.mult))

            def dilated_part(p_):
                d = [u for u, (kind, _, _) in enumerate(UNITS) if kind == DIL]
                for tile in range(TILES):
                    wait_moved(dve, T[("pv", d[p_], tile)])
                v = o_dil[p_].rearrange("p t (h n) -> p (t h) n", h=HPG)
                link(nc.vector.tensor_tensor(v, v, dilw[:, 5, p_].unsqueeze(2).broadcast_to([P, 8, HEAD]), ALU.mult))
                if p_ == 1:
                    link(nc.vector.tensor_tensor(o_b, o_dil[0], o_dil[1], ALU.add))
                if p_ == 2:
                    nc.vector.tensor_tensor(o_b, o_b, o_dil[2], ALU.add).then_inc(ob_ready, 1)

            last_pv = pl.at[("pv", len(UNITS) - 1, 1)] + LAG
            for pos in range(MIX_SLOTS):
                if pos >= 3:
                    split_slot(dve, mix_slot, 0, 0, pos)
                if 2 <= pos < 10:
                    x_pairs("mix", pos - 2)
                if pos == 21:
                    dve.wait_ge(wg_rounded, 1)
                    nc.vector.tensor_tensor(wg_lo[:, :, :], wg_raw, wg_hi[:, :, :].bitcast(F32), ALU.subtract) \
                        .then_inc(wg_split, 1)
                if pos in (25, 31):
                    v = (pos - 25) // 6
                    dve.wait_ge(blk_rounded, v + 1)
                    nc.vector.tensor_tensor(blk_lo[:, v], blk[:, :, :, :].rearrange("p j g n -> p j (g n)"),
                                            blk_hi[:, v].bitcast(F32), ALU.subtract).then_inc(blk_split, 1)
                order, end = divmod(pos - LAG, 8)
                if end == 7 and order >= 0:
                    kind, col = MIX_ORDER[order]
                    c = mix_acc + order
                    if kind != "gate":
                        wait_acc_full(dve, mix_slot + 8 * (order + 1))
                    if kind == "cmp":
                        src = acc_pair(c)[:, :, 0:GROUPS * N_CMP]
                        nc.vector.tensor_copy(cx[:, col, 0], src).then_inc(acc_emptied[c % 2], 1)
                        dve.wait_ge(acc_emptied[c % 2], c // 2 + 1)
                        link(nc.vector.tensor_tensor(cx[:, col, 1], cx[:, col, 0], cx[:, col, 0], ALU.mult))
                        link(nc.vector.tensor_scalar(cx[:, col, 1], cx[:, col, 1], 0.044715, 1.0, ALU.mult, ALU.add))
                        nc.vector.tensor_tensor(cx[:, col, 1], cx[:, col, 1], cx[:, col, 0], ALU.mult).then_inc(gelu_in, 1)
                    elif kind != "gate":
                        nc.vector.tensor_copy(chunk_buf(order), acc_pair(c)).then_inc(acc_emptied[c % 2], 1)
                if pos >= LAG + 2:
                    order, end = divmod(pos - LAG - 2, 8)
                    if end == 7 and MIX_ORDER[order][0] == "cmp":
                        col = MIX_ORDER[order][1]
                        dve.wait_ge(gelu_tanh, col + 1)
                        nc.vector.scalar_tensor_tensor(cx[:, col, 3], cx[:, col, 2], 1.0, cx[:, col, 0], ALU.add,
                                                       ALU.mult).then_inc(gelu_out, 1)
                for name in pl.by_pos.get(pos - LAG, ()):
                    t = T[name]
                    if name[0] == "s":
                        mask_scores(name, t)
                    elif name[0] == "pT":
                        _, u, j = name
                        wait_filled(dve, t)
                        if u:
                            wait_filled(dve, T[("pv", u - 1, 1)])
                        if UNITS[u][0] == CMP:
                            nc.vector.tensor_copy(pT[0:N_CMP, j], bank[0:N_CMP, t.bank, :]
                                                  .rearrange("p (h n) -> p h n", h=HPG)) \
                                .then_inc(bank_emptied[t.bank], 1)
                        else:
                            nc.vector.tensor_copy(pT[:, j], bank[:, t.bank, :].rearrange("p (h n) -> p h n", h=HPG)) \
                                .then_inc(bank_emptied[t.bank], 1)
                    elif name[0] == "pv" and UNITS[name[1]][0] != DIL:
                        add_values(name, t)
                    elif name[0] == "oT":
                        j = name[1]
                        split_pair(dve, name, pair_of(oT_lo, 2 * j), pair_of(oT_hi, 2 * j))
                    elif name[0] == "gates":
                        wait_moved(dve, t)
                        nc.vector.tensor_scalar(gates[:, :, :], gates[:, :, :], 0.5, 0.5, ALU.mult, ALU.add) \
                            .then_inc(gates_ready, 1)
                        dve.wait_ge(gates_ready, 1)
                if pos in max_at:
                    maxima(max_at[pos])
                if pos - 2 in max_at and UNITS[max_at[pos - 2]][0] == CMP:
                    u = max_at[pos - 2]
                    dve.wait_ge(probs_ready, exps_before[u + 1])
                    v = s0[:, 0, 0:8 * N_CMP].rearrange("p (e n) -> p e n", e=8)
                    link(nc.vector.tensor_reduce(sums[:, u, :], v, AX_X, ALU.add))
                if pos == last_pv + 1:
                    dilated_shift()
                if pos == last_pv + 3:
                    dilated_merge()
                if last_pv + 4 <= pos < last_pv + 7:
                    dilated_part(pos - last_pv - 4)

            merges = [0]

            def merge_chunk(n):
                first = len(MIX_ORDER) - 8
                ca, cb = ab_acc + 2 * n, ab_acc + 2 * n + 1
                u_, v_ = rot_tmp, (rot_q, rot_k)[n % 2]
                dve.wait_ge(slots_used, tail_slot + 6 * (n + 1))
                if n == 0:
                    dve.wait_ge(acc_emptied[(mix_acc + len(MIX_ORDER) - 1) % 2], (mix_acc + len(MIX_ORDER) - 1) // 2 + 1)
                if n >= 2:
                    wait_filled(dve, T[("m", n - 2, 1)])
                nc.vector.scalar_tensor_tensor(u_[:, :, :], chunk_buf(first + n), 1.0, acc_pair(ca), ALU.add,
                                               ALU.mult).then_inc(acc_emptied[0], 1)
                nc.vector.scalar_tensor_tensor(v_[:, :, :], chunk_buf(first + 4 + n), 1.0, acc_pair(cb), ALU.add,
                                               ALU.mult).then_inc(acc_emptied[1], 1)
                dve.wait_ge(acc_emptied[0], ca // 2 + 1)
                dve.wait_ge(acc_emptied[1], cb // 2 + 1)
                nc.vector.tensor_tensor(v_[:, :, :], u_[:, :, :], v_[:, :, :], ALU.add).then_inc(merged, 1)
                dve.wait_ge(merged, n + 1)

            for pos in range(TAIL_SLOTS):
                split_slot(dve, tail_slot, 0, 0, pos)
                if pos >= LAG and (pos - LAG) % 6 == 5 and (pos - LAG) // 6 < OUT_CHUNKS:
                    merge_chunk((pos - LAG) // 6)
                for d in range(2):
                    if pos - LAG - d in merge_at:
                        n = merge_at[pos - LAG - d]
                        kt = 4 * n + 2 * d
                        split_pair(dve, ("m", n, d), pair_of(act_lo, kt), pair_of(act_hi, kt), 0.5)
                o_pos = pos - 6 * OUT_CHUNKS - LAG
                if o_pos >= 0 and o_pos % 8 == 7:
                    c = o_pos // 8
                    if c == 0:
                        dve.wait_ge(resid_ready, 2)
                    add_chunk_static(c)

            for s in range(3):
                split_slot(dve, gu_slot[1], 0, 0, s)
            add_chunk_static(OUT_CHUNKS - 1)
            layer_norm(1)
            gu_chunk(1, 0, True)
            with dve.Fori(1, GU_CHUNKS) as i:
                gu_chunk(1, i, False)
            up_half(1, GU_CHUNKS)
            for half in range(2):
                split_h(1, GU_CHUNKS, half)
            down(1)
            layer_norm(2)
            dve.wait_ge(ln_nat_loaded, 3 * 32)
            dve.wait_ge(z_dve, 6)
            v = resid[:, 0, :]
            link(nc.vector.tensor_tensor(v, v, ln_nat[:, 0, :], ALU.mult))
            nc.vector.tensor_tensor(v, v, ln_nat[:, 1, :], ALU.add).then_inc(out_ready, 1)

        @block.tensor
        def _(pe):
            def x_task(f, j):
                t = T[("x", f, j)]
                if f == 0:
                    if j == 0:
                        pe.wait_ge(small_loaded, 16)
                        pe.wait_ge(x_loaded[0], 16)
                        pe.wait_ge(x_loaded[1], 16)
                else:
                    ln = 2 if f == 1 else 1
                    half = (j // 4) + 1
                    if j % 4 == 0:
                        pe.wait_ge(z_dve, 2 * (ln - 1) + half)
                        pe.wait_ge(z_act, 2 * (ln - 1) + half)
                wait_bank_free(pe, t)
                transpose_pair(resid, 2 * P * j, t.bank)

            def first_chunk(f, n0, c0):
                wait_acc_free(pe, c0, 0, 2, 0)
                for j in range(3):
                    x_task(f, j)
                for s in range(GU_SLOTS):
                    if s + 3 < GU_SLOTS:
                        x_task(f, s + 3)
                    input_ready(f, s)
                    multiply_slot(pe, act_hi, act_lo, 2 * s, c0 % 2, s == 0, s == GU_SLOTS - 1, n0, 0, 0, s)

            def input_ready(f, j):
                t = T[("x", f, j)]
                if f == 0:
                    wait_moved(pe, t)
                else:
                    pe.wait_ge(lo_pairs, (0 if f == "mix" else 8) + j + 1)

            def h_task(f, i, half):
                t = T[("h", f, 0, half)]
                if half == 0:
                    pe.wait_ge(acc_emptied[1], i + (gu_acc[f] // 2))
                if not (isinstance(i, int) and i - 1 + t.use == 0):
                    pe.wait_ge(bank_emptied[half], i + (t.use - 1))
                transpose_pair(hid, 2 * P * half, half)

            def gu_chunk(f, i, peel):
                n0, per, c0 = gu_slot[f], 2 * GU_SLOTS, gu_acc[f]
                for h in range(2):
                    if peel and h == 0:
                        first_chunk(f, n0, c0)
                        if f == 0:
                            setup_task()
                        continue
                    wait_acc_free(pe, c0, i, 2, h)
                    for s in range(GU_SLOTS):
                        multiply_slot(pe, act_hi, act_lo, 2 * s, h, s == 0, s == GU_SLOTS - 1, n0, i, per,
                                      h * GU_SLOTS + s)
                        if not peel and h == 0 and s in (3, 4):
                            h_task(f, i, s - 3)

            def setup_task():
                t = T[("setup",)]
                pe.wait_ge(consts_loaded, 16 * 6)
                wait_bank_free(pe, t)
                nc.tensor.transpose(bank[:, t.bank, 0:64], vec_rows[:, :], ident[0:64, 0:64])
                nc.tensor.transpose(bank[:, t.bank, 64:96], pos_rows[:, 0, :], ident[0:32, 0:32])
                nc.tensor.transpose(bank[:, t.bank, 96:128], pos_rows[:, 1, :], ident[0:32, 0:32]).then_inc(bank_filled, 1)

            def ffn(f):
                gu_chunk(f, 0, True)
                with pe.Fori(1, GU_CHUNKS) as i:
                    gu_chunk(f, i, False)
                for half in range(2):
                    h_task(f, GU_CHUNKS, half)
                for half in range(2):
                    wait_moved(pe, T[("h", f, GU_CHUNKS - 1, half)])
                with pe.Fori(0, 2) as i:
                    for c in range(2):
                        wait_acc_free(pe, down_acc[f], i, 2, c)
                        for s in range(DOWN_SLOTS):
                            multiply_slot(pe, hT_hi, hT_lo, 2 * s, (down_acc[f] + c) % 2, s == 0, s == DOWN_SLOTS - 1,
                                          down_slot[f], i, 2 * DOWN_SLOTS, c * DOWN_SLOTS + s)

            ffn(0)

            def buffered(eng_order):
                c = mix_acc + eng_order
                pe.wait_ge(acc_emptied[c % 2], c // 2 + 1)

            def heads_T(src, t):
                wait_bank_free(pe, t)
                for h, v in enumerate(src):
                    mm = nc.tensor.transpose(bank[:, t.bank, h * P:(h + 1) * P], v, ident)
                mm.then_inc(bank_filled, 1)

            def gate_products(t):
                pe.wait_ge(wg_split, 1)
                wait_bank_free(pe, t)
                for tile in range(TILES):
                    o = bank[:, t.bank, tile * NSA_GATES:(tile + 1) * NSA_GATES]
                    for k in range(KT):
                        ah, al = (a[:, k, tile * P:(tile + 1) * P] for a in (act_hi, act_lo))
                        nc.tensor.matmul(o, ah, wg_hi[:, k, :], start=k == 0, stop=False)
                        nc.tensor.matmul(o, ah, wg_lo[:, k, :], start=False, stop=False)
                        mm = nc.tensor.matmul(o, al, wg_hi[:, k, :], start=False, stop=k == KT - 1)
                mm.then_inc(bank_filled, 1)

            def cmp_out(name, t):
                v = int(name[0] == "vcmp")
                pe.wait_ge(gelu_out, v + 1)
                pe.wait_ge(cw2_loaded, 32)
                wait_bank_free(pe, t)
                g_ = cx[:, v, 3]
                if v == 0:
                    for k in range(2):
                        mm = nc.tensor.matmul(bank[:, t.bank, 0:GROUPS * N_CMP], cw2[:, 0, k, :], g_[:, k, :],
                                              start=k == 0, stop=k == 1)
                else:
                    for g in range(GROUPS):
                        for k in range(2):
                            mm = nc.tensor.matmul(bank[0:N_CMP, t.bank, g * HEAD:(g + 1) * HEAD],
                                                  g_[:, k, g * N_CMP:(g + 1) * N_CMP], cw2[:, 1, k, :],
                                                  start=k == 0, stop=k == 1)
                mm.then_inc(bank_filled, 1)

            def queries(name, t):
                _, u, tile = name
                kind, g, _ = UNITS[u]
                if kind == CMP:
                    buffered(3 + g)
                    src = chunk_buf(3 + g)
                else:
                    pe.wait_ge(roped, 2 + g if kind == SLC else 4 + 2 * g)
                    src = rot_q
                heads_T([src[:, tile, h * HEAD:(h + 1) * HEAD] for h in range(HPG)], t)

            def keys(name, t):
                _, u, tile = name
                kind, g, _ = UNITS[u]
                pe.wait_ge(roped, 1 if kind == SLC else 5 + 2 * g)
                heads_T([rot_k[:, tile, h * HEAD:(h + 1) * HEAD] for h in range(HPG)], t)

            def scores(name, t):
                _, u, j = name
                kind, g, _ = UNITS[u]
                owner = u - 1 if kind == WINDOW else u
                for tile in range(TILES):
                    wait_moved(pe, T[("qT", owner, tile)])
                if kind in (SLC, WINDOW):
                    for tile in range(TILES):
                        wait_moved(pe, T[("kT", 0, tile)])
                if kind == DIL:
                    for tile in range(TILES):
                        wait_moved(pe, T[("kT", u, tile)])
                if kind == CMP:
                    wait_moved(pe, T[("kcmp",)])
                wait_bank_free(pe, t)

                def key(h, lo, hi):
                    if kind == DIL:
                        return kT[:, h, lo:hi]
                    return kT[:, (0 if kind == SLC else 2) + g, lo:hi]

                if kind == CMP:
                    for tile in range(TILES):
                        for h in range(HPG):
                            e = tile * HPG + h
                            mm = nc.tensor.matmul(bank[:, t.bank, e * N_CMP:(e + 1) * N_CMP], qT[:, h, tile * P:(tile + 1) * P],
                                                  kcmpT[:, g * N_CMP:(g + 1) * N_CMP], start=True, stop=True)
                elif j < 2:
                    for h in range(2 * j, 2 * j + 2):
                        o = (h - 2 * j) * TOKENS
                        mm = nc.tensor.matmul(bank[:, t.bank, o:o + TOKENS], qT[:, h, P:TOKENS], key(h, 0, TOKENS),
                                              start=True, stop=True)
                else:
                    for h in range(HPG):
                        mm = nc.tensor.matmul(bank[:, t.bank, h * P:(h + 1) * P], qT[:, h, 0:P], key(h, 0, P),
                                              start=True, stop=True)
                mm.then_inc(bank_filled, 1)

            def probs_T(name, t):
                _, u, j = name
                pe.wait_ge(probs_ready, exps_before[u + 1])
                wait_bank_free(pe, t)
                if UNITS[u][0] == CMP:
                    for h in range(HPG):
                        e = j * HPG + h
                        mm = nc.tensor.transpose(bank[0:N_CMP, t.bank, h * P:(h + 1) * P],
                                                 s0[:, 0, e * N_CMP:(e + 1) * N_CMP], ident)
                else:
                    for h in range(HPG):
                        v = s1[:, h, j * P:(j + 1) * P] if j < 2 else s0[:, h, :]
                        mm = nc.tensor.transpose(bank[:, t.bank, h * P:(h + 1) * P], v, ident)
                mm.then_inc(bank_filled, 1)

            def values(name, t):
                _, u, tile = name
                kind, g, _ = UNITS[u]
                for j in range(2 if kind == CMP else 3):
                    wait_moved(pe, T[("pT", u, j)])
                if kind == CMP:
                    wait_moved(pe, T[("vcmp",)])
                elif kind == DIL:
                    buffered(9 + 3 * g)
                else:
                    buffered(1 if kind == SLC else 2)
                wait_bank_free(pe, t)
                for h in range(HPG):
                    o = bank[:, t.bank, h * P:(h + 1) * P]
                    if kind == CMP:
                        mm = nc.tensor.matmul(o, pT[0:N_CMP, tile, h, :], vcmp[:, g, :], start=True, stop=True)
                        continue
                    if kind == DIL:
                        v, c0 = chunk_buf(9 + 3 * g), h * HEAD
                    else:
                        v, c0 = chunk_buf(1 if kind == SLC else 2), 256 + g * HEAD
                    parts = [(2, 0)] if tile == 0 else [(0, 0), (1, 1)]
                    for n, (j, kt) in enumerate(parts):
                        mm = nc.tensor.matmul(o, pT[:, j, h, :], v[:, kt, c0:c0 + HEAD], start=n == 0,
                                              stop=n == len(parts) - 1)
                mm.then_inc(bank_filled, 1)

            def bank_task(name):
                t = T[name]
                if name[0] == "kcT" or name[0] == "vcT":
                    buffered(0)
                    wait_bank_free(pe, t)
                    transpose_pair(chunk_buf(0), 256 * int(name[0] == "vcT"), t.bank)
                elif name[0] == "gates":
                    gate_products(t)
                elif name[0] in ("kcmp", "vcmp"):
                    cmp_out(name, t)
                elif name[0] == "qT":
                    queries(name, t)
                elif name[0] == "kT":
                    keys(name, t)
                elif name[0] == "s":
                    scores(name, t)
                elif name[0] == "pT":
                    probs_T(name, t)
                elif name[0] == "pv":
                    values(name, t)
                elif name[0] == "oT":
                    j = name[1]
                    if j < 4:
                        pe.wait_ge(o_ready, 8)
                    else:
                        pe.wait_ge(ob_ready, 1)
                    wait_bank_free(pe, t)
                    if j < 4:
                        transpose_pair(o_a, 2 * P * j, t.bank)
                    else:
                        transpose_pair(o_b, 2 * P * (j - 4), t.bank)

            def cmp_slot(v, s, n):
                r = n % RING
                pe.wait_ge(lo_done, n + 1)
                for k in range(4):
                    b_hi, b_lo = blk_hi[:, v, 4 * s + k, :], blk_lo[:, v, 4 * s + k, :]
                    first, last = s == 0 and k == 0, s == CMP_SLOTS - 1 and k == 3
                    for half in range(2):
                        o = acc[:, 2 * (acc_of(v) % 2) + half, 0:GROUPS * N_CMP]
                        c = k * CMP_HIDDEN + half * P
                        hi, lo = w_hi[:, r, c:c + P], w_lo[:, r, c:c + P]
                        nc.tensor.matmul(o, hi, b_hi, start=first, stop=False)
                        nc.tensor.matmul(o, hi, b_lo, start=False, stop=False)
                        mm = nc.tensor.matmul(o, lo, b_hi, start=False, stop=last)
                mm.then_inc(slots_used, 1)

            def acc_of(v):
                return mix_acc + 5 + v

            for order, (kind, col) in enumerate(MIX_ORDER):
                c = mix_acc + order
                if order:
                    wait_acc_free(pe, c, 0, 2, 0)
                if kind == "cmp":
                    pe.wait_ge(blk_split, col + 1)
                for s in range(8):
                    pos = 8 * order + s
                    if order == 0:
                        if s == 0:
                            wait_acc_free(pe, c, 0, 2, 0)
                            for j in range(3):
                                x_task("mix", j)
                        if s + 3 < GU_SLOTS:
                            x_task("mix", s + 3)
                        input_ready("mix", s)
                    if kind == "cmp":
                        cmp_slot(col, s, mix_slot + pos)
                    else:
                        multiply_slot(pe, act_hi, act_lo, 2 * s, c % 2, s == 0, s == 7, mix_slot, 0, 0, pos)
                    for name in pl.by_pos.get(pos, ()):
                        bank_task(name)

            def merge_tasks(pos):
                for d in range(2):
                    if pos - d in merge_at:
                        n = merge_at[pos - d]
                        t = T[("m", n, d)]
                        if d == 0:
                            pe.wait_ge(merged, n + 1)
                        wait_bank_free(pe, t)
                        transpose_pair((rot_q, rot_k)[n % 2], 2 * P * d, t.bank)

            pos = 0
            for n in range(OUT_CHUNKS):
                for part, (ns, kt0) in enumerate(((4, 0), (2, 8))):
                    c = ab_acc + 2 * n + part
                    wait_acc_free(pe, c, 0, 2, 0)
                    if n == 0:
                        for j in (range(4) if part == 0 else range(4, 6)):
                            wait_moved(pe, T[("oT", j)])
                    for s in range(ns):
                        multiply_slot(pe, oT_hi, oT_lo, kt0 + 2 * s, c % 2, s == 0, s == ns - 1, tail_slot, 0, 0, pos)
                        merge_tasks(pos)
                        pos += 1
            for n in range(OUT_CHUNKS):
                c = o_acc + n
                wait_acc_free(pe, c, 0, 2, 0)
                for s in range(8):
                    if n == 0:
                        wait_moved(pe, T[("m", s // 2, s % 2)])
                    multiply_slot(pe, act_hi, act_lo, 2 * s, c % 2, s == 0, s == 7, tail_slot, 0, 0, pos)
                    merge_tasks(pos)
                    pos += 1

            ffn(1)

        @block.gpsimd
        def _(pool):
            steps = [0]

            def link(ins):
                steps[0] += 1
                ins.then_inc(pool_step, 1)
                pool.wait_ge(pool_step, steps[0])

            def residual(which):
                wait_filled(pool, T[("x", 0, 7) if which == 0 else ("x", "mix", 7) if which == 1 else ("x", 1, 7)])
                if which == 0:
                    nc.gpsimd.tensor_scalar(resid[:, :, :], resid[:, :, :], ALPHA, None, ALU.mult).then_inc(resid_ready, 1)
                    return
                pool.wait_ge(ln_nat_loaded, 32 * which)
                link(nc.gpsimd.tensor_scalar(ln_nat[:, :, :], ln_nat[:, :, :], ALPHA, None, ALU.mult))
                for tile in range(TILES):
                    link(nc.gpsimd.tensor_tensor(resid[:, tile, :], resid[:, tile, :], ln_nat[:, 0, :], ALU.mult))
                link(nc.gpsimd.tensor_tensor(resid[:, 0, :], resid[:, 0, :], ln_nat[:, 1, :], ALU.add))
                nc.gpsimd.tensor_tensor(resid[:, 1, :], resid[:, 1, :], ln_nat[:, 1, :], ALU.add).then_inc(resid_ready, 1)

            def rotate(src, dst, tmp, heads):
                cos = rope[:, 0].unsqueeze(2).broadcast_to([P, TILES, heads, HEAD])
                sin_a = rope[:, 1, :, 0:64].unsqueeze(2).broadcast_to([P, TILES, heads, 64])
                sin_b = rope[:, 1, :, 64:128].unsqueeze(2).broadcast_to([P, TILES, heads, 64])
                s_, d_, t_ = (v.rearrange("p t (h n) -> p t h n", n=HEAD) for v in (src, dst, tmp))
                link(nc.gpsimd.tensor_tensor(t_[:, :, :, 0:64], s_[:, :, :, 64:128], sin_a, ALU.mult))
                link(nc.gpsimd.tensor_tensor(t_[:, :, :, 64:128], s_[:, :, :, 0:64], sin_b, ALU.mult))
                link(nc.gpsimd.tensor_tensor(d_, s_, cos, ALU.mult))
                return d_, t_

            def projected(order):
                c = mix_acc + order
                pool.wait_ge(acc_emptied[c % 2], c // 2 + 1)

            jobs = [0]

            def rotate_job(parts, dst, readers):
                for r in readers:
                    wait_filled(pool, T[r])
                at = 0
                for n, (order, lo, hi) in enumerate(parts):
                    projected(order)
                    w = hi - lo
                    d_, t_ = rotate(chunk_buf(order)[:, :, lo:hi], dst[:, :, at:at + w], rot_tmp[:, :, at:at + w], w // HEAD)
                    ins = nc.gpsimd.tensor_tensor(d_, d_, t_, ALU.add)
                    if n < len(parts) - 1:
                        link(ins)
                    at += w
                ins.then_inc(roped, 1)
                jobs[0] += 1
                pool.wait_ge(roped, jobs[0])

            residual(0)
            residual(1)
            for v in range(2):
                wait_moved(pool, T[("kcT",) if v == 0 else ("vcT",)])
                if v:
                    pool.wait_ge(blk_split, 1)
                for g in range(GROUPS):
                    windows = kcvcT[:, v, g, :].rearrange("p (m r) -> p r m", r=CMP_STRIDE)
                    for a in range(2):
                        js = slice(16 * a, 16 * a + 16)
                        ins = nc.gpsimd.tensor_tensor(
                            blk[:, js, g, :], windows[:, :, a:a + N_CMP],
                            posT[:, v, js].unsqueeze(2).broadcast_to([P, 16, N_CMP]), ALU.add)
                        if (g, a) != (1, 1):
                            link(ins)
                ins.then_inc(blk_ready, 1)
            pool.wait_ge(mix_consts_loaded, 48)
            rotate_job([(1, 0, 256), (2, 0, 256)], rot_k, [])
            rotate_job([(3, 0, 512)], rot_q, [])
            rotate_job([(4, 0, 512)], rot_q, [("qT", 0, 1)])
            for p_ in range(3):
                u = 6 + p_
                prev_q = ("qT", 2, 1) if p_ == 0 else ("qT", u - 1, 1)
                prev_k = ("kT", 0, 1) if p_ == 0 else ("kT", u - 1, 1)
                rotate_job([(7 + 3 * p_, 0, 512)], rot_q, [prev_q])
                rotate_job([(8 + 3 * p_, 0, 512)], rot_k, [prev_k])
            residual(2)
            pool.wait_ge(ln_nat_loaded, 96)
            pool.wait_ge(z_act, 6)
            v = resid[:, 1, :]
            link(nc.gpsimd.tensor_tensor(v, v, ln_nat[:, 0, :], ALU.mult))
            nc.gpsimd.tensor_tensor(v, v, ln_nat[:, 1, :], ALU.add).then_inc(out_ready_pool, 1)


_INS = ["x", "ffn1_w_gate", "ffn1_w_up", "ffn1_w_down", "ln_ffn1_g", "ln_ffn1_b", "w_in", "cmp_k_pos", "cmp_k_w1",
        "cmp_k_w2", "cmp_v_pos", "cmp_v_w1", "cmp_v_w2", "w_branch_a", "w_branch_b", "w_o", "ln_mix_g", "ln_mix_b",
        "ffn2_w_gate", "ffn2_w_up", "ffn2_w_down", "ln_ffn2_g", "ln_ffn2_b"]


def kernel(**inputs):
    import concourse.bacc as bacc
    from concourse.bass_utils import run_bass_kernel_spmd

    nc = bacc.Bacc("TRN2", target_bir_lowering=False, num_devices=1, dynamic_dma_scratch_size=1024)
    named = [(name, np.ascontiguousarray(inputs[name])) for name in _INS]
    named += list(zip(("rope", "masks", "small"), mixer_constants()))
    arrays, args = {}, []
    for name, a in named:
        arrays[f"in_{name}_dram"] = a
        args.append(nc.dram_tensor(f"in_{name}_dram", a.shape, mybir.dt.from_np(a.dtype), kind="ExternalInput").ap())
    out = nc.dram_tensor("out_dram", (1, TOKENS, D), F32, kind="ExternalOutput").ap()
    build(nc, *args, out)
    r = run_bass_kernel_spmd(nc, [arrays], core_ids=[0])
    return r.results[0]["out_dram"]
```

```python
from contextlib import ExitStack

import numpy as np
import concourse.bass as bass
from concourse import mybir

F32 = mybir.dt.float32
F32R = mybir.dt.float32r
ALU = mybir.AluOpType
ACT = mybir.ActivationFunctionType
AX_X = mybir.AxisListType.X

P = 128
D = 2048
TOKENS = 256
TILES = TOKENS // P
HEAD = 128
HIDDEN = 5632
COLS = 512
KT = D // P
FT = HIDDEN // P
RING = 4
SLOT_KT = 2
SLOT = SLOT_KT * COLS
LAG = 2
BANKS = 4
OUT_PIECES = ((0, 1024), (0, 512), (512, 1280), (1280, D))
WARM_START, WARM_H, WARM_LN = 2, 4, 6
ALPHA = 2.0 ** 0.25
EPS = 1e-5
SCALE = HEAD ** -0.5
MASKED = -1e30

GU_CHUNKS = HIDDEN // COLS
GU_SLOTS = KT // SLOT_KT
DOWN_SLOTS = FT // SLOT_KT
OUT_CHUNKS = D // COLS

GROUPS = 2
HPG = 4
NSA_HEADS = GROUPS * HPG
CMP_BLOCK, CMP_STRIDE = 32, 16
N_CMP = (TOKENS - CMP_BLOCK) // CMP_STRIDE + 1
CMP_HIDDEN = 2 * HEAD
CMP_SLOTS = CMP_BLOCK // 4
N_BLK = GROUPS * N_CMP
WIDE = 66
PATTERNS = ((128, 1), (512, 4), (2048, 16))
NSA_GATES = NSA_HEADS * 3
W_GATE0 = 2560
GELU_C = (2.0 / np.pi) ** 0.5

DIL0 = W_GATE0 + NSA_GATES
MIX_ORDER = [("kv", 1024), ("kv", 1536), ("kv", 2048), ("q", 0), ("q", 512), ("cmp", 0), ("cmp", 1)]
for _p in range(3):
    MIX_ORDER += [("q", DIL0 + _p * 512), ("k", DIL0 + 1536 + _p * 512), ("v", DIL0 + 3072 + _p * 512)]
MIX_ORDER += [("gate", DIL0 + 4608 + _n * 512) for _n in range(8)]
CHUNK_BUF = [0, 1, 2, 3, 4, None, None, 5, 6, 7, 8, 9, 10, 11, 12, 13, 0, 1, 2, 5, 6, 7, 3, 4]
MIX_SLOTS = 8 * len(MIX_ORDER)
SLC, WINDOW, CMP, DIL = range(4)
Z_PIECES = ((0, 256), (256, 1024), (1024, 2048))
UNITS = [(SLC, 0, 44), (WINDOW, 0, 0), (SLC, 1, 0), (WINDOW, 1, 0), (CMP, 0, 0), (CMP, 1, 0),
         (DIL, 0, 86), (DIL, 1, 106), (DIL, 2, 131)]


class Plan:

    def __init__(self):
        self.k, self.uses, self.t, self.at, self.by_pos = 0, [0] * BANKS, {}, {}, {}


class Task:

    def __init__(self, k, bank_, use):
        self.k, self.bank, self.use = k, bank_, use


def plan():
    pl = Plan()

    def task(name, bank=None):
        b = pl.k % BANKS if bank is None else bank
        pl.t[name] = Task(pl.k, b, pl.uses[b])
        pl.k += 1
        pl.uses[b] += 1

    def ffn(f):
        for j in range(GU_SLOTS):
            task(("x", f, j), j % BANKS)
        if f == 0:
            task(("setup",), 2)
        for i in range(GU_CHUNKS):
            for half in range(2):
                task(("h", f, i, half), half)

    ffn(0)
    for j in range(GU_SLOTS):
        task(("x", "mix", j), j % BANKS)

    busy = set()

    def place(name, earliest):
        pos = earliest
        while pos in busy:
            pos += 1
        busy.add(pos)
        pl.at[name] = pos
        return pos

    place(("kcT",), 10)
    place(("vcT",), 11)
    place(("gates",), 24)
    place(("gatesT",), 30)
    place(("hidT", 0), 53)
    place(("kcmp",), 58)
    place(("hidT", 1), 61)
    place(("vcmp",), 66)
    scored = probs_read = pv_read = 0
    for u, (kind, g, ready) in enumerate(UNITS):
        first = max(ready, scored + 1)
        last = first
        if kind != WINDOW:
            for tile in range(TILES):
                last = place(("qT", u, tile), max(first, last))
        if kind == DIL or (kind == SLC and g == 0):
            for tile in range(TILES):
                last = place(("kT", u, tile), last)
        n_scores = 1 if kind == CMP else 3
        earliest = max(last + 5 if kind != WINDOW else scored + 1, probs_read - 1)
        for j in range(n_scores):
            earliest = place(("s", u, j), earliest)
        scored = earliest
        n_probs = 2 if kind == CMP else 3
        earliest = max(scored + 8, pv_read - 1)
        for j in range(n_probs):
            earliest = place(("pT", u, j), earliest)
        probs_read = earliest
        earliest += 5
        for tile in range(TILES):
            earliest = place(("pv", u, tile), earliest)
        pv_read = earliest
    for j in range(4):
        place(("oT", j), pv_read + 3)
    for j in range(2):
        place(("oT", 4 + j), pv_read + 11)
    assert max(busy) < MIX_SLOTS, max(busy)
    for name in sorted(pl.at, key=pl.at.get):
        task(name)
    for name, pos in pl.at.items():
        pl.by_pos.setdefault(pos, []).append(name)
    for n in range(OUT_CHUNKS):
        for half in range(2):
            task(("m", n, half))
    ffn(1)
    return pl


def mixer_constants():
    inv = (np.float32(10000.0) ** (-np.arange(0, HEAD, 2, dtype=np.float32) / np.float32(HEAD))).astype(np.float32)
    ang = np.arange(TOKENS, dtype=np.float32)[:, None] * inv[None, :]
    cos, sin = np.cos(ang), np.sin(ang)
    rope = np.stack([np.concatenate([cos, cos], 1), np.concatenate([-sin, sin], 1)])
    rope = rope.reshape(2, TILES, P, HEAD).transpose(2, 0, 1, 3)
    t, k = np.arange(P)[:, None] + P, np.arange(TOKENS)[None, :]
    masks = []
    for win, dil in ((TOKENS, 1),) + PATTERNS:
        d = t - k
        masks.append((d >= 0) & (d <= win) & (d % dil == 0))
    masks = np.where(np.stack(masks, 1), 0.0, MASKED)
    tt = np.arange(TOKENS)
    seen = (np.arange(N_CMP) * CMP_STRIDE + CMP_BLOCK - 1)[None, :] <= tt[:, None]
    cmask = np.where(seen, 0.0, MASKED).reshape(TILES, P, N_CMP).transpose(1, 0, 2)
    any_seen = seen.any(1).astype(np.float32).reshape(TILES, P).T
    small = np.concatenate([cmask.reshape(P, -1), any_seen, np.eye(P)], 1)
    return (np.ascontiguousarray(rope, np.float32), np.ascontiguousarray(masks, np.float32),
            np.ascontiguousarray(small, np.float32))


def build(nc, x, w1_gate, w1_up, w1_down, ln1_g, ln1_b, w_in, ck_pos, ck_w1, ck_w2, cv_pos, cv_w1, cv_w2,
          w_a, w_b, w_o, ln2_g, ln2_b, w2_gate, w2_up, w2_down, ln3_g, ln3_b, rope_c, masks_c, small_c, out):
    (w1_gate, w1_up, w1_down, ln1_g, ln1_b, w_in, ck_pos, ck_w1, ck_w2, cv_pos, cv_w1, cv_w2, w_a, w_b, w_o,
     ln2_g, ln2_b, w2_gate, w2_up, w2_down, ln3_g, ln3_b) = (
        a[0] for a in (w1_gate, w1_up, w1_down, ln1_g, ln1_b, w_in, ck_pos, ck_w1, ck_w2, cv_pos, cv_w1, cv_w2,
                       w_a, w_b, w_o, ln2_g, ln2_b, w2_gate, w2_up, w2_down, ln3_g, ln3_b))
    pl = plan()
    T = pl.t
    ctx = ExitStack()
    with ctx:
        def sb(name, shape, dt=F32, stack=ctx):
            return stack.enter_context(nc.sbuf_tensor(name, shape, dt))

        def sem(name):
            return ctx.enter_context(nc.semaphore(name))

        raw = sb("raw", [P, RING, SLOT])
        w_hi = sb("w_hi", [P, RING, SLOT], F32R)
        w_lo = sb("w_lo", [P, RING, SLOT], F32R)
        act_hi = sb("act_hi", [P, KT, TOKENS], F32R)
        act_lo = sb("act_lo", [P, KT, TOKENS], F32R)
        resid = sb("resid", [P, TILES, D])
        ln_nat = sb("ln_nat", [P, 2, D])
        over = ExitStack()
        gelu_x = sb("gelu_x", [N_BLK, 2, CMP_HIDDEN], F32, over)
        hidT = sb("hidT", [P, 2, 2, N_BLK], F32, over)
        kcmpT = sb("kcmpT", [P, GROUPS * N_CMP], F32, over)
        vcmp = sb("vcmp", [N_CMP, GROUPS, HEAD], F32, over)
        gates = sb("gates", [P, TILES, NSA_GATES], F32, over)
        coef = sb("coef", [P, 2, 8], F32, over)
        over.close()
        affine = sb("affine", [P, 2, 2, TOKENS])
        small = sb("small", [P, TILES * N_CMP + TILES + P])
        vec_rows = sb("vec_rows", [64, P])
        pos_rows = sb("pos_rows", [CMP_BLOCK, 2, P])
        vecT = sb("vecT", [P, 4 * KT + 2 * CMP_BLOCK])
        stats = sb("stats", [P, TILES, OUT_CHUNKS, 6])
        ln_s = sb("ln_s", [P, 8, TILES])
        mv = sb("mv", [P, TILES, 2])
        over = ExitStack()
        hT_hi = sb("hT_hi", [P, FT, TOKENS], F32R, over)
        hT_lo = sb("hT_lo", [P, FT, TOKENS], F32R, over)
        gate_t = sb("gate_t", [P, TILES, COLS], F32, over)
        hid = sb("hid", [P, TILES, COLS], F32, over)
        over.close()
        chunks_lo = sb("chunks_lo", [P, 8, TILES, COLS])
        over = ExitStack()
        oT_hi = sb("oT_hi", [P, 12, TOKENS], F32R, over)
        oT_lo = sb("oT_lo", [P, 12, TOKENS], F32R, over)
        over.close()
        over = ExitStack()
        kcvcT = sb("kcvcT", [P, 2, GROUPS, TOKENS], F32, over)
        blk = sb("blk", [P, CMP_BLOCK, GROUPS, N_CMP], F32, over)
        blk_hi = sb("blk_hi", [P, 2, (CMP_BLOCK - 1) * N_BLK + WIDE], F32R, over)
        blk_lo = sb("blk_lo", [P, 2, (CMP_BLOCK - 1) * N_BLK + WIDE], F32R, over)
        over.close()
        chunks_hi = sb("chunks_hi", [P, 6, TILES, COLS])
        rot_q = sb("rot_q", [P, TILES, COLS])
        rot_k = sb("rot_k", [P, TILES, COLS])
        rot_tmp = sb("rot_tmp", [P, TILES, COLS])
        qT = sb("qT", [P, HPG, TOKENS])
        kT = sb("kT", [P, HPG, TOKENS])
        over = ExitStack()
        wg_hi = sb("wg_hi", [P, (KT - 1) * NSA_GATES + WIDE], F32R, over)
        wg_lo = sb("wg_lo", [P, (KT - 1) * NSA_GATES + WIDE], F32R, over)
        over.close()
        s0 = sb("s0", [P, HPG, P])
        s1 = sb("s1", [P, HPG, TOKENS])
        pT = sb("pT", [P, 3, HPG, P])
        o_a = sb("o_a", [P, TILES, NSA_HEADS * HEAD])
        rope = sb("rope", [P, 2, TILES, HEAD])
        masks = sb("masks", [P, 4, TOKENS])
        wg_raw = o_a[:, 0, 0:KT * NSA_GATES]
        gatesT = pos_rows[0:NSA_GATES].rearrange("j v n -> j (v n)")
        negmax = sb("negmax", [P, len(UNITS), 8])
        sums = sb("sums", [P, len(UNITS), 8])
        dilw = sb("dilw", [P, 6, 3, 8])

        def chunk_buf(order):
            b = CHUNK_BUF[order]
            return chunks_lo[:, b] if b < 8 else chunks_hi[:, b - 8]

        o_dil = [ln_nat[:, 0, 0:1024], ln_nat[:, 0, 1024:2048], ln_nat[:, 1, 0:1024]]
        o_dil = [v.rearrange("p (t n) -> p t n", t=TILES) for v in o_dil]
        o_b = ln_nat[:, 1, 1024:2048].rearrange("p (t n) -> p t n", t=TILES)
        o_add = ln_nat[:, 1, 1024:1536].rearrange("p (h n) -> p h n", h=HPG)
        cw2 = ln_nat[:, 1, 1536:2048].rearrange("p (v k n) -> p v k n", v=2, k=2)
        cmp_mask = small[:, 0:TILES * N_CMP].rearrange("p (t n) -> p t n", t=TILES)
        any_seen = small[:, TILES * N_CMP:TILES * N_CMP + TILES]
        ident = small[:, TILES * N_CMP + TILES:]
        posT = vecT[:, 4 * KT:].rearrange("p (v j) -> p v j", v=2)

        acc = ctx.enter_context(nc.psum_tensor("acc", [P, 4, 512], F32))
        bank = ctx.enter_context(nc.psum_tensor("bank", [P, BANKS, 512], F32))

        raw_loaded = [sem(f"raw_loaded{r}") for r in range(RING)]
        hi_done = sem("hi_done")
        lo_done = sem("lo_done")
        slots_used = sem("slots_used")
        acc_emptied = [sem("acc_emptied0"), sem("acc_emptied1")]
        bank_filled = sem("bank_filled")
        bank_emptied = [sem(f"bank_emptied{b}") for b in range(BANKS)]
        hi_moved = sem("hi_moved")
        x_loaded = [sem(f"x_loaded{q}") for q in range(4)]
        small_loaded = sem("small_loaded")
        consts_loaded = sem("consts_loaded")
        mix_consts_loaded = sem("mix_consts_loaded")
        cw2_loaded = sem("cw2_loaded")
        ln_nat_loaded = sem("ln_nat_loaded")
        resid_ready = sem("resid_ready")
        gate_tanh = sem("gate_tanh")
        var_ready = sem("var_ready")
        std_ready = sem("std_ready")
        norm_ready = sem("norm_ready")
        z_dve = sem("z_dve")
        z_act = sem("z_act")
        lo_pairs = sem("lo_pairs")
        stats_done = sem("stats_done")
        roped = sem("roped")
        blk_ready = sem("blk_ready")
        blk_rounded = sem("blk_rounded")
        blk_split = sem("blk_split")
        gelu_in = sem("gelu_in")
        gelu_tanh = sem("gelu_tanh")
        gelu_out = sem("gelu_out")
        pads_zeroed = sem("pads_zeroed")
        wg_rounded = sem("wg_rounded")
        wg_split = sem("wg_split")
        max_ready = sem("max_ready")
        probs_ready = sem("probs_ready")
        o_ready = sem("o_ready")
        dil_shift = sem("dil_shift")
        dil_exp = sem("dil_exp")
        ob_ready = sem("ob_ready")
        merged = sem("merged")
        dve_step = sem("dve_step")
        pool_step = sem("pool_step")
        out_ready = sem("out_ready")
        out_ready_pool = sem("out_ready_pool")
        stored = sem("stored")
        tile0_full = sem("tile0_full")
        zeros_ready = sem("zeros_ready")

        gu_slot = [0, 0]
        down_slot = [GU_CHUNKS * 2 * GU_SLOTS, 0]
        mix_slot = down_slot[0] + OUT_CHUNKS * DOWN_SLOTS
        tail_slot = mix_slot + MIX_SLOTS
        TAIL_SLOTS = OUT_CHUNKS * 6 + OUT_CHUNKS * GU_SLOTS
        gu_slot[1] = tail_slot + TAIL_SLOTS
        down_slot[1] = gu_slot[1] + GU_CHUNKS * 2 * GU_SLOTS
        ahead, x_from = [0, 3], [0, 2]
        gu_acc = [0, 0]
        down_acc = [2 * GU_CHUNKS, 0]
        mix_acc = down_acc[0] + OUT_CHUNKS
        ab_acc = mix_acc + len(MIX_ORDER)
        o_acc = ab_acc + 2 * OUT_CHUNKS
        gu_acc[1] = o_acc + OUT_CHUNKS
        down_acc[1] = gu_acc[1] + 2 * GU_CHUNKS
        assert all(v % 4 == 0 for v in (*gu_slot, *down_slot, mix_slot, tail_slot))
        assert all(v % 2 == 0 for v in (*gu_acc, *down_acc, mix_acc, ab_acc, o_acc))

        def ring_turn(n0, i, per, s):
            return i * (per // RING) + (n0 + s) // RING + 1

        def load_slot(sp, src, n0, i, per, s):
            if not (isinstance(i, int) and n0 + i * per + s < RING):
                sp.wait_ge(lo_done, i * per + (n0 + s - RING + 1))
            r = (n0 + s) % RING
            dst = raw[:, r, :].rearrange("p (t n) -> p t n", n=src.shape[2])
            sp.dma_start(dst, src).then_inc(raw_loaded[r], 16)

        def round_slot(act, n0, i, per, s):
            r = (n0 + s) % RING
            act.wait_ge(raw_loaded[r], ring_turn(n0, i, per, s) * 16)
            if not (isinstance(i, int) and n0 + i * per + s < RING):
                act.wait_ge(slots_used, i * per + (n0 + s - RING + 1))
            nc.scalar.activation(w_hi[:, r, :], raw[:, r, :], ACT.Copy).then_inc(hi_done, 1)

        def split_slot(dve, n0, i, per, s):
            r = (n0 + s) % RING
            dve.wait_ge(hi_done, i * per + (n0 + s + 1))
            nc.vector.tensor_tensor(w_lo[:, r, :], raw[:, r, :], w_hi[:, r, :].bitcast(F32),
                                    ALU.subtract).then_inc(lo_done, 1)

        def multiply_slot(pe, a_hi, a_lo, kt0, pair, first, last, n0, i, per, s, tiles=range(TILES)):
            r = (n0 + s) % RING
            pe.wait_ge(lo_done, i * per + (n0 + s + 1))
            for k in range(SLOT_KT):
                hi = w_hi[:, r, k * COLS:(k + 1) * COLS]
                lo = w_lo[:, r, k * COLS:(k + 1) * COLS]
                for tile in tiles:
                    o = acc[:, 2 * pair + tile, :]
                    ah = a_hi[:, kt0 + k, tile * P:(tile + 1) * P]
                    al = a_lo[:, kt0 + k, tile * P:(tile + 1) * P]
                    nc.tensor.matmul(o, ah, hi, start=first and k == 0, stop=False)
                    nc.tensor.matmul(o, ah, lo, start=False, stop=False)
                    mm = nc.tensor.matmul(o, al, hi, start=False, stop=last and k == SLOT_KT - 1)
            if TILES - 1 in tiles:
                mm.then_inc(slots_used, 1)
            elif last:
                mm.then_inc(tile0_full, 1)

        def wait_acc_full(eng, slot_end):
            eng.wait_ge(slots_used, slot_end)

        def wait_acc_free(pe, c0, i, per, c):
            if not (isinstance(i, int) and c0 + i * per + c < 2):
                pe.wait_ge(acc_emptied[(c0 + c) % 2], i * (per // 2) + (c0 + c) // 2)

        def acc_pair(c):
            return acc[:, 2 * (c % 2):2 * (c % 2) + 2, :]

        def wait_filled(eng, t):
            eng.wait_ge(bank_filled, t.k + 1)

        def wait_bank_free(pe, t):
            if t.use:
                pe.wait_ge(bank_emptied[t.bank], t.use)

        def wait_moved(eng, t):
            eng.wait_ge(bank_emptied[t.bank], t.use + 1)

        def transpose_pair(src, col, b):
            for k in range(2):
                for tile in range(TILES):
                    mm = nc.tensor.transpose(bank[:, b, k * TOKENS + tile * P:k * TOKENS + (tile + 1) * P],
                                             src[:, tile, col + k * P:col + (k + 1) * P], ident)
            mm.then_inc(bank_filled, 1)

        moved = {}
        n_hi = 0
        hi_order = [("x", 0, j) for j in range(8)]
        hi_order += [("h", 0, i, half) for i in range(GU_CHUNKS) for half in range(2)]
        hi_order += [("x", "mix", j) for j in range(8)]
        hi_order += [("oT", j) for j in range(6)]
        hi_order += [("m", n, half) for n in range(OUT_CHUNKS) for half in range(2)]
        hi_order += [("x", 1, j) for j in range(8)]
        hi_order += [("h", 1, i, half) for i in range(GU_CHUNKS) for half in range(2)]
        for name in hi_order:
            moved[name] = n_hi
            n_hi += 1

        def pair_of(t_, kt):
            return t_[:, kt:kt + 2, :].rearrange("p k n -> p (k n)")

        def round_pair(act, name, dst, scale=1.0):
            t = T[name]
            wait_filled(act, t)
            nc.scalar.activation(dst, bank[:, t.bank, :], ACT.Copy, scale=scale).then_inc(hi_moved, 1)

        def split_pair(dve, name, dst, hi, scale=1.0):
            t = T[name]
            dve.wait_ge(hi_moved, moved[name] + 1)
            nc.vector.scalar_tensor_tensor(dst, bank[:, t.bank, :], scale, hi.bitcast(F32), ALU.mult,
                                           ALU.subtract).then_inc(bank_emptied[t.bank], 1)

        w_gu = [(w1_gate, w1_up), (w2_gate, w2_up)]
        w_dn = [w1_down, w2_down]

        def rows(w):
            return w.rearrange("(t p) n -> p t n", p=P)

        def bank_use(name, i):
            return i + T[name].use

        mix_src = []
        for kind, col in MIX_ORDER:
            for s in range(8):
                if kind == "cmp":
                    w = (ck_w1, cv_w1)[col]
                    mix_src.append(rows(w)[:, 4 * s:4 * s + 4, :])
                else:
                    mix_src.append(rows(w_in)[:, 2 * s:2 * s + 2, col:col + COLS])
        for n in range(OUT_CHUNKS):
            for w, ns in ((w_a, 4), (w_b, 2)):
                mix_src += [rows(w)[:, 2 * s:2 * s + 2, n * COLS:(n + 1) * COLS] for s in range(ns)]
        for n in range(OUT_CHUNKS):
            mix_src += [rows(w_o)[:, 2 * s:2 * s + 2, n * COLS:(n + 1) * COLS] for s in range(8)]
        assert len(mix_src) == MIX_SLOTS + TAIL_SLOTS

        merge_at = {6 * n + 5 + 3: n for n in range(OUT_CHUNKS)}

        def gate_chunk(act, order):
            wait_acc_full(act, mix_slot + 8 * (order + 1))
            b = CHUNK_BUF[order]
            last = ("pv", 3, 1) if b < 3 else ("pv", 6, 1) if b >= 5 else ("qT", 5, 1)
            wait_filled(act, T[last])
            nc.scalar.activation(chunk_buf(order), acc_pair(mix_acc + order), ACT.Tanh, scale=0.5) \
                .then_inc(acc_emptied[(mix_acc + order) % 2], 1)

        def move_heads(act, name, t):
            u = name[1]
            wait_filled(act, t)
            src = bank[:, t.bank, :].rearrange("p (h n) -> p h n", n=P)
            dst = qT if name[0] == "qT" else kT
            nc.scalar.activation(dst[:, :, name[2] * P:(name[2] + 1) * P], src, ACT.Copy) \
                .then_inc(bank_emptied[t.bank], 1)

        n_exps = [1 if kind == CMP else 2 * HPG for kind, _, _ in UNITS]
        exps_before = [sum(n_exps[:u]) for u in range(len(UNITS) + 1)]

        def exponentials(act, u):
            kind = UNITS[u][0]
            act.wait_ge(max_ready, u + 1)
            if kind == CMP:
                v = s0[:, 0, 0:8 * N_CMP]
                nc.scalar.activation(v, v, ACT.Exp, scale=SCALE).then_inc(probs_ready, 1)
                return
            for e in range(2 * HPG):
                v = s0[:, e] if e < HPG else s1[:, e - HPG]
                nc.scalar.activation(v, v, ACT.Exp, bias=negmax[:, u, e:e + 1], scale=SCALE,
                                     accum_out=sums[:, u, e:e + 1]).then_inc(probs_ready, 1)

        block = ctx.enter_context(nc.Block())

        @block.sync
        def _(sp):
            def load_x(q):
                cs = slice(q * COLS, (q + 1) * COLS)
                sp.dma_start(resid[:, :, cs], x[0].rearrange("(t p) d -> p t d", p=P)[:, :, cs]) \
                    .then_inc(x_loaded[q], 16)

            load_x(0)
            sp.dma_start(small[:, :], small_c).then_inc(small_loaded, 16)

            def gu_chunk(f, i):
                for h in range(2):
                    for s in range(GU_SLOTS):
                        src = rows(w_gu[f][h])[:, 2 * s:2 * s + 2, bass.ds(i * COLS, COLS)]
                        load_slot(sp, src, gu_slot[f], i, 2 * GU_SLOTS, h * GU_SLOTS + s)
                        if f == 0 and isinstance(i, int) and h == 0:
                            if s < 3:
                                load_x(s + 1)
                            if s == 4:
                                load_vectors()

            def load_vectors():
                for v, a in enumerate((ln1_g, ln1_b, ln2_g, ln2_b)):
                    sp.dma_start(vec_rows[16 * v:16 * v + 16, :], a.rearrange("(t p) -> t p", p=P)) \
                        .then_inc(consts_loaded, 16)
                sp.dma_start(pos_rows[:, 0, :], ck_pos).then_inc(consts_loaded, 16)
                sp.dma_start(pos_rows[:, 1, :], cv_pos).then_inc(consts_loaded, 16)

            def ffn(f):
                gu_chunk(f, 0)
                if f == 0:
                    load_ln(0)
                with sp.Fori(1, GU_CHUNKS) as i:
                    gu_chunk(f, i)
                if f == 1:
                    sp.wait_ge(resid_ready, 3)
                    load_ln(2)
                with sp.Fori(0, 2) as i:
                    for c in range(2):
                        for s in range(DOWN_SLOTS):
                            src = rows(w_dn[f])[:, 2 * s:2 * s + 2, bass.ds(i * (2 * COLS) + c * COLS, COLS)]
                            load_slot(sp, src, down_slot[f], i, 2 * DOWN_SLOTS, c * DOWN_SLOTS + s)

            def load_ln(which):
                g, b = ((ln1_g, ln1_b), (ln2_g, ln2_b), (ln3_g, ln3_b))[which]
                for v, a in enumerate((g, b)):
                    sp.dma_start(ln_nat[:, v, :], a.rearrange("(a n) -> a n", a=1).broadcast_to([P, D])) \
                        .then_inc(ln_nat_loaded, 16)

            ffn(0)
            for pos in range(MIX_SLOTS + TAIL_SLOTS):
                load_slot(sp, mix_src[pos], mix_slot, 0, 0, pos)
                if pos == 4:
                    sp.wait_ge(slots_used, mix_slot)
                    sp.dma_start(rope[:, :, :, :], rope_c).then_inc(mix_consts_loaded, 16)
                    sp.dma_start(masks[:, :, :], masks_c).then_inc(mix_consts_loaded, 16)
                    sp.dma_start(wg_raw.rearrange("p (t n) -> p t n", n=NSA_GATES),
                                 rows(w_in)[:, :, W_GATE0:W_GATE0 + NSA_GATES]) \
                        .then_inc(mix_consts_loaded, 16)
                if pos == 32:
                    sp.wait_ge(resid_ready, 2)
                    for v, w in enumerate((ck_w2, cv_w2)):
                        sp.dma_start(cw2[:, v, :, :], w.rearrange("(t p) n -> p t n", p=P)) \
                            .then_inc(cw2_loaded, 16)
                if pos == MIX_SLOTS + 8:
                    wait_filled(sp, T[("oT", 5)])
                    load_ln(1)

            ffn(1)
            out_t = out[0].rearrange("(t p) d -> p t d", p=P)
            pieces = ((0, (1024, D), out_ready, 1), (0, OUT_PIECES[0], out_ready_pool, 1), (1, OUT_PIECES[2], out_ready, 2),
                      (1, OUT_PIECES[1], out_ready_pool, 2), (1, OUT_PIECES[3], out_ready, 3))
            for tile, (lo, hi), ready, n in pieces:
                sp.wait_ge(ready, n)
                sp.dma_start(out_t[:, tile, lo:hi], resid[:, tile, lo:hi]).then_inc(stored, 16)
            sp.wait_ge(stored, 16 * len(pieces))

        @block.scalar
        def _(act):
            def gu_chunk(f, i, peel):
                per, c0 = 2 * GU_SLOTS, gu_acc[f]
                for s in range(2 * GU_SLOTS):
                    if not (peel and s < ahead[f]):
                        round_slot(act, gu_slot[f], i, per, s)
                    if peel and 0 <= s - x_from[f] < 8:
                        x_pairs(f, s - x_from[f])
                    if s == GU_SLOTS - 1 + LAG:
                        act.wait_ge(slots_used, i * per + (gu_slot[f] + GU_SLOTS))
                        if not (peel and f == 0):
                            act.wait_ge(acc_emptied[1], i + (c0 // 2))
                        nc.scalar.activation(gate_t[:, :, :], acc_pair(0), ACT.Tanh, scale=0.5).then_inc(gate_tanh, 1)
                    if not peel and s in (5, 6):
                        round_h(f, i, s - 5)

            def round_h(f, i, half):
                t = T[("h", f, 0, half)]
                act.wait_ge(bank_filled, i * 2 + (t.k + 1 - 2))
                dst = hT_hi[:, bass.ds(i * 4 + (2 * half - 4), 2), :] if not isinstance(i, int) else \
                    hT_hi[:, i * 4 + 2 * half - 4:i * 4 + 2 * half - 2, :]
                nc.scalar.activation(dst, bank[:, half, :].rearrange("p (k n) -> p k n", k=2), ACT.Copy).then_inc(hi_moved, 1)

            def x_pairs(f, j):
                if f == 0:
                    round_pair(act, ("x", 0, j), pair_of(act_hi, 2 * j))
                else:
                    ln, t = 1 if f == 1 else 0, T[("x", f, j)]
                    wait_filled(act, t)
                    if ln or j >= 2:
                        act.wait_ge(lo_pairs, 8 * ln + max(j - 1, 0))
                    for k in range(2):
                        at = 32 * ln + 2 * j + k
                        ins = nc.scalar.activation(affine[:, j % 2, k], bank[:, t.bank, k * TOKENS:(k + 1) * TOKENS],
                                                   ACT.Identity, bias=vecT[:, at + 16:at + 17], scale=vecT[:, at:at + 1])
                    ins.then_inc(bank_emptied[t.bank], 1)
                    wait_moved(act, t)
                    nc.scalar.activation(pair_of(act_hi, 2 * j), affine[:, j % 2].rearrange("p k n -> p (k n)"),
                                         ACT.Copy).then_inc(hi_moved, 1)

            def down(f):
                if f == 0:
                    with act.Fori(0, 2) as i:
                        for s in range(2 * DOWN_SLOTS):
                            round_slot(act, down_slot[0], i, 2 * DOWN_SLOTS, s + 3)
                else:
                    for s in range(3, OUT_CHUNKS * DOWN_SLOTS):
                        round_slot(act, down_slot[1], 0, 0, s)

            def layer_norm_act(which):
                act.wait_ge(var_ready, which + 1)
                nc.scalar.activation(ln_s[:, 1, :], ln_s[:, 0, :], ACT.Sqrt).then_inc(std_ready, 1)
                act.wait_ge(norm_ready, which + 1)
                for lo, hi in Z_PIECES:
                    v = resid[:, 1, lo:hi]
                    nc.scalar.activation(v, v, ACT.Identity, bias=ln_s[:, 4, 1:2], scale=ln_s[:, 3, 1:2]).then_inc(z_act, 1)

            gu_chunk(0, 0, True)
            with act.Fori(1, GU_CHUNKS) as i:
                gu_chunk(0, i, False)
            for s in range(3):
                round_slot(act, down_slot[0], 0, 0, s)
            for half in range(2):
                round_h(0, GU_CHUNKS, half)
            down(0)

            exp_at, dil_at = {}, None
            for u, (kind, g, _) in enumerate(UNITS):
                exp_at[pl.at[("s", u, 0 if kind == CMP else 2)] + LAG + 1] = u
            layer_norm_act(0)
            for pos in range(MIX_SLOTS):
                if pos >= 3:
                    round_slot(act, mix_slot, 0, 0, pos)
                if 2 <= pos < 10:
                    x_pairs("mix", pos - 2)
                if pos == 17:
                    act.wait_ge(mix_consts_loaded, 48)
                    nc.scalar.activation(wg_hi[:, 0:KT * NSA_GATES], wg_raw, ACT.Copy).then_inc(wg_rounded, 1)
                if pos in (24, 30):
                    v = (pos - 24) // 6
                    act.wait_ge(blk_ready, v + 1)
                    nc.scalar.activation(blk_hi[:, v, 0:CMP_BLOCK * N_BLK], blk[:, :, :, :].rearrange("p j g n -> p (j g n)"),
                                         ACT.Copy).then_inc(blk_rounded, 1)
                order, end = divmod(pos - LAG, 8)
                if end == 7 and order >= 0:
                    kind, col = MIX_ORDER[order]
                    if kind == "cmp":
                        act.wait_ge(gelu_in, col + 1)
                        nc.scalar.activation(gelu_x[:, 1], gelu_x[:, 1], ACT.Tanh, scale=GELU_C).then_inc(gelu_tanh, 1)
                    if kind == "gate":
                        gate_chunk(act, order)
                for name in pl.by_pos.get(pos - LAG, ()):
                    t = T[name]
                    if name[0] in ("kcT", "vcT"):
                        wait_filled(act, t)
                        nc.scalar.activation(kcvcT[:, int(name[0] == "vcT")].rearrange("p g n -> p (g n)"),
                                             bank[:, t.bank, :], ACT.Copy).then_inc(bank_emptied[t.bank], 1)
                    elif name[0] == "gates":
                        wait_filled(act, t)
                        nc.scalar.activation(gatesT, bank[0:NSA_GATES, t.bank, 0:TOKENS], ACT.Tanh, scale=0.5) \
                            .then_inc(bank_emptied[t.bank], 1)
                    elif name[0] == "hidT":
                        wait_filled(act, t)
                        nc.scalar.activation(hidT[:, name[1]].rearrange("p k n -> p (k n)"), bank[:, t.bank, 0:2 * N_BLK],
                                             ACT.Copy).then_inc(bank_emptied[t.bank], 1)
                    elif name[0] == "kcmp":
                        wait_filled(act, t)
                        nc.scalar.activation(kcmpT[:, :], bank[:, t.bank, 0:GROUPS * N_CMP], ACT.Copy, scale=0.5) \
                            .then_inc(bank_emptied[t.bank], 1)
                    elif name[0] == "vcmp":
                        wait_filled(act, t)
                        nc.scalar.activation(vcmp[:, :, :], bank[0:N_CMP, t.bank, 0:GROUPS * HEAD]
                                             .rearrange("p (g n) -> p g n", g=GROUPS), ACT.Copy, scale=0.5) \
                            .then_inc(bank_emptied[t.bank], 1)
                    elif name[0] in ("qT", "kT"):
                        move_heads(act, name, t)
                    elif name[0] == "pv" and UNITS[name[1]][0] == DIL:
                        wait_filled(act, t)
                        p_ = UNITS[name[1]][1]
                        act.wait_ge(resid_ready, 2)
                        nc.scalar.activation(o_dil[p_][:, name[2], :], bank[:, t.bank, :], ACT.Copy) \
                            .then_inc(bank_emptied[t.bank], 1)
                    elif name[0] == "oT":
                        round_pair(act, name, pair_of(oT_hi, 2 * name[1]))
                if pos in exp_at:
                    exponentials(act, exp_at[pos])
                if pos == pl.at[("pv", len(UNITS) - 1, 1)] + LAG + 2:
                    act.wait_ge(dil_shift, 1)
                    nc.scalar.activation(dilw[:, 1], dilw[:, 0], ACT.Exp).then_inc(dil_exp, 1)

            for pos in range(TAIL_SLOTS):
                round_slot(act, tail_slot, 0, 0, pos)
                if pos == LAG - 1:
                    gate_chunk(act, len(MIX_ORDER) - 1)
                for d in range(2):
                    if pos - LAG - d in merge_at:
                        n = merge_at[pos - LAG - d]
                        round_pair(act, ("m", n, d), pair_of(act_hi, 4 * n + 2 * d), 0.5)

            for s in range(3):
                round_slot(act, gu_slot[1], 0, 0, s)
            layer_norm_act(1)
            gu_chunk(1, 0, True)
            with act.Fori(1, GU_CHUNKS) as i:
                gu_chunk(1, i, False)
            for s in range(3):
                round_slot(act, down_slot[1], 0, 0, s)
            for half in range(2):
                round_h(1, GU_CHUNKS, half)
            down(1)
            for tile in range(TILES):
                at = slice(tile, tile + 1)
                act.wait_ge(var_ready, 3 + tile)
                nc.scalar.activation(ln_s[:, 1, at], ln_s[:, 0, at], ACT.Sqrt).then_inc(std_ready, 1)
                act.wait_ge(norm_ready, 3 + tile)
                for lo, hi in OUT_PIECES[:1] if tile == 0 else OUT_PIECES[1:]:
                    v = resid[:, tile, lo:hi]
                    nc.scalar.activation(v, v, ACT.Identity, bias=ln_s[:, 4, at], scale=ln_s[:, 3, at]).then_inc(z_act, 1)

        @block.vector
        def _(dve):
            steps = [0]

            def link(ins):
                steps[0] += 1
                ins.then_inc(dve_step, 1)
                dve.wait_ge(dve_step, steps[0])

            def gu_chunk(f, i, peel):
                per = 2 * GU_SLOTS
                for s in range(2 * GU_SLOTS):
                    if not (peel and s < ahead[f]):
                        split_slot(dve, gu_slot[f], i, per, s)
                    if peel and 0 <= s - x_from[f] < 8:
                        x_pairs(f, s - x_from[f])
                    if f == 0 and peel and s == 11:
                        t = T[("setup",)]
                        wait_filled(dve, t)
                        nc.vector.tensor_copy(vecT[:, :], bank[:, t.bank, 0:128]).then_inc(bank_emptied[t.bank], 1)
                    if not peel and s == 1:
                        up_half(f, i)
                    if not peel and s in (5, 6):
                        split_h(f, i, s - 5)
                    if s == GU_SLOTS - 1 + LAG:
                        dve.wait_ge(gate_tanh, i + (GU_CHUNKS * f + 1))
                        nc.vector.scalar_tensor_tensor(gate_t[:, :, :], gate_t[:, :, :], 1.0, acc_pair(0), ALU.add,
                                                       ALU.mult).then_inc(acc_emptied[0], 1)

            def up_half(f, i):
                per, c0 = 2 * GU_SLOTS, gu_acc[f]
                dve.wait_ge(slots_used, i * per + gu_slot[f])
                dve.wait_ge(acc_emptied[0], i + (c0 // 2))
                if not (isinstance(i, int) and i == 1):
                    dve.wait_ge(bank_filled, i * 2 + (T[("h", f, 0, 0)].k - 2))
                nc.vector.tensor_tensor(hid[:, :, :], gate_t[:, :, :], acc_pair(1), ALU.mult).then_inc(acc_emptied[1], 1)

            def split_h(f, i, half):
                dve.wait_ge(hi_moved, i * 2 + (moved[("h", f, 0, half)] + 1 - 2))
                if isinstance(i, int):
                    k0 = slice(i * 4 + 2 * half - 4, i * 4 + 2 * half - 2)
                else:
                    k0 = bass.ds(i * 4 + (2 * half - 4), 2)
                nc.vector.tensor_tensor(hT_lo[:, k0, :], bank[:, half, :].rearrange("p (k n) -> p k n", k=2),
                                        hT_hi[:, k0, :].bitcast(F32), ALU.subtract).then_inc(bank_emptied[half], 1)

            def x_pairs(f, j):
                if f == 0:
                    split_pair(dve, ("x", 0, j), pair_of(act_lo, 2 * j), pair_of(act_hi, 2 * j))
                    return
                name = ("x", f, j)
                ln = 1 if f == 1 else 0
                dve.wait_ge(hi_moved, moved[name] + 1)
                nc.vector.tensor_tensor(pair_of(act_lo, 2 * j), affine[:, j % 2].rearrange("p k n -> p (k n)"),
                                        pair_of(act_hi, 2 * j).bitcast(F32), ALU.subtract).then_inc(lo_pairs, 1)
                dve.wait_ge(lo_pairs, 8 * ln + j + 1)

            def add_chunk(f, i, c, scale, n_slots, slot0, acc0):
                col = i * (2 * COLS) + c * COLS
                cs = slice(col, col + COLS) if isinstance(i, int) else bass.ds(col, COLS)
                pair = (acc0 + c) % 2
                dve.wait_ge(slots_used, i * (2 * n_slots) + (slot0 + (c + 1) * n_slots))
                nc.vector.scalar_tensor_tensor(resid[:, :, cs], acc_pair(pair), scale, resid[:, :, cs], ALU.mult,
                                               ALU.add).then_inc(acc_emptied[pair], 1)
                dve.wait_ge(acc_emptied[pair], i + ((acc0 + c) // 2 + 1))
                for tile in range(TILES):
                    nc.vector.bn_stats(stats[:, tile, bass.ds(i * 2 + c, 1), :].rearrange("p a b -> p (a b)")
                                       if not isinstance(i, int) else stats[:, tile, i * 2 + c, :],
                                       resid[:, tile, cs]).then_inc(stats_done, 1)

            def last_chunk_tile(tile):
                if tile == 0:
                    dve.wait_ge(tile0_full, OUT_CHUNKS)
                else:
                    dve.wait_ge(slots_used, down_slot[1] + OUT_CHUNKS * DOWN_SLOTS)
                c, at, n = OUT_CHUNKS - 1, slice(tile, tile + 1), 3 + tile
                v = resid[:, tile, c * COLS:(c + 1) * COLS]
                o = acc[:, 2 * ((down_acc[1] + c) % 2) + tile, :]
                link(nc.vector.scalar_tensor_tensor(v, o, 0.25, v, ALU.mult, ALU.add))
                link(nc.vector.bn_stats(stats[:, tile, c, :], v))
                link(nc.vector.bn_aggr(mv[:, tile, :], stats[:, tile, :, :]))
                nc.vector.tensor_scalar(ln_s[:, 0, at], mv[:, tile, 1:2], EPS, None, ALU.add).then_inc(var_ready, 1)
                dve.wait_ge(std_ready, n)
                inverse_deviation(at)
                nc.vector.scalar_tensor_tensor(ln_s[:, 4, at], mv[:, tile, 0:1], -1.0, ln_s[:, 3, at], ALU.mult,
                                               ALU.mult).then_inc(norm_ready, 1)
                dve.wait_ge(norm_ready, n)

            def inverse_deviation(at=slice(0, TILES)):
                link(nc.vector.reciprocal(ln_s[:, 2, at], ln_s[:, 1, at]))
                link(nc.vector.tensor_tensor(ln_s[:, 5, at], ln_s[:, 2, at], ln_s[:, 2, at], ALU.mult))
                link(nc.vector.tensor_tensor(ln_s[:, 5, at], ln_s[:, 5, at], ln_s[:, 0, at], ALU.mult))
                link(nc.vector.tensor_scalar(ln_s[:, 5, at], ln_s[:, 5, at], -0.5, 1.5, ALU.mult, ALU.add))
                link(nc.vector.tensor_tensor(ln_s[:, 3, at], ln_s[:, 2, at], ln_s[:, 5, at], ALU.mult))

            def add_chunk_static(c):
                add_chunk(None, 0, c, 1.0, 8, tail_slot + 6 * OUT_CHUNKS, o_acc)

            def down(f):
                dve.wait_ge(resid_ready, 1 if f == 0 else 3)
                if f == 0:
                    with dve.Fori(0, 2) as i:
                        for s in range(2 * DOWN_SLOTS):
                            split_slot(dve, down_slot[0], i, 2 * DOWN_SLOTS, s + 3)
                            if s % DOWN_SLOTS == DOWN_SLOTS - 1:
                                add_chunk(0, i, s // DOWN_SLOTS, 0.25, DOWN_SLOTS, down_slot[0], down_acc[0])
                    return
                for i in range(2):
                    for s in range(2 * DOWN_SLOTS):
                        if i * 2 * DOWN_SLOTS + s + 3 < OUT_CHUNKS * DOWN_SLOTS:
                            split_slot(dve, down_slot[1], i, 2 * DOWN_SLOTS, s + 3)
                        if s % DOWN_SLOTS == DOWN_SLOTS - 1 and (i, s) != (1, 2 * DOWN_SLOTS - 1):
                            add_chunk(1, i, s // DOWN_SLOTS, 0.25, DOWN_SLOTS, down_slot[1], down_acc[1])

            def layer_norm(which):
                dve.wait_ge(stats_done, 8 * (which + 1))
                for tile in range(TILES):
                    link(nc.vector.bn_aggr(mv[:, tile, :], stats[:, tile, :, :]))
                nc.vector.tensor_scalar(ln_s[:, 0, :], mv[:, :, 1], EPS, None, ALU.add).then_inc(var_ready, 1)
                dve.wait_ge(std_ready, which + 1)
                inverse_deviation()
                nc.vector.scalar_tensor_tensor(ln_s[:, 4, :], mv[:, :, 0], -1.0, ln_s[:, 3, :], ALU.mult,
                                               ALU.mult).then_inc(norm_ready, 1)
                dve.wait_ge(norm_ready, which + 1)
                for lo, hi in Z_PIECES:
                    v = resid[:, 0, lo:hi]
                    nc.vector.tensor_scalar(v, v, ln_s[:, 3, 0:1], ln_s[:, 4, 0:1], ALU.mult, ALU.add).then_inc(z_dve, 1)

            nc.vector.memset(hid[:, 0, :], 0.0).then_inc(zeros_ready, 1)
            gu_chunk(0, 0, True)
            with dve.Fori(1, GU_CHUNKS) as i:
                gu_chunk(0, i, False)
            up_half(0, GU_CHUNKS)
            for s in range(3):
                split_slot(dve, down_slot[0], 0, 0, s)
            for half in range(2):
                split_h(0, GU_CHUNKS, half)
            down(0)

            layer_norm(0)
            max_at = {}
            for u, (kind, g, _) in enumerate(UNITS):
                max_at[pl.at[("s", u, 0 if kind == CMP else 2)] + LAG] = u
            unit_out = [0]

            def mask_scores(name, t):
                _, u, j = name
                kind, g, _ = UNITS[u]
                wait_filled(dve, t)
                if u:
                    last = max(T[("pT", u - 1, jj)].k for jj in range(2 if UNITS[u - 1][0] == CMP else 3))
                    dve.wait_ge(bank_filled, last + 1)
                m = 0 if kind != DIL else 1 + g
                if kind == CMP:
                    src = bank[:, t.bank, 0:8 * N_CMP].rearrange("p (t h n) -> p t h n", t=TILES, h=HPG)
                    dst = s0[:, 0, 0:8 * N_CMP].rearrange("p (t h n) -> p t h n", t=TILES, h=HPG)
                    msk = cmp_mask.unsqueeze(2).broadcast_to([P, TILES, HPG, N_CMP])
                elif j < 2:
                    src = bank[:, t.bank, :].rearrange("p (h n) -> p h n", h=2)
                    dst = s1[:, 2 * j:2 * j + 2, :]
                    msk = masks[:, m, :].unsqueeze(1).broadcast_to([P, 2, TOKENS])
                else:
                    src = bank[:, t.bank, :].rearrange("p (h n) -> p h n", h=HPG)
                    dst = s0[:, :, :]
                    msk = masks[:, m, P:TOKENS].unsqueeze(1).broadcast_to([P, HPG, P])
                nc.vector.tensor_tensor(dst, src, msk, ALU.add).then_inc(bank_emptied[t.bank], 1)

            def maxima(u):
                kind = UNITS[u][0]
                for j in range(1 if kind == CMP else 3):
                    wait_moved(dve, T[("s", u, j)])
                if kind == CMP:
                    v = s0[:, 0, 0:8 * N_CMP].rearrange("p (e n) -> p e n", e=8)
                    link(nc.vector.tensor_reduce(negmax[:, u, :], v, AX_X, ALU.max))
                    nc.vector.tensor_tensor(v, v, negmax[:, u, :].unsqueeze(2).broadcast_to([P, 8, N_CMP]),
                                            ALU.subtract).then_inc(max_ready, 1)
                    return
                link(nc.vector.tensor_reduce(negmax[:, u, 0:HPG], s0[:, :, :], AX_X, ALU.max))
                link(nc.vector.tensor_reduce(negmax[:, u, HPG:2 * HPG], s1[:, :, :], AX_X, ALU.max))
                nc.vector.tensor_scalar(negmax[:, u, :], negmax[:, u, :], -SCALE, None, ALU.mult).then_inc(max_ready, 1)

            def coefficients(u):
                kind, g, _ = UNITS[u]
                dve.wait_ge(probs_ready, exps_before[u + 1])
                link(nc.vector.reciprocal(coef[:, 0, :], sums[:, u, :]))
                branch = {CMP: 0, SLC: 1, WINDOW: 2}[kind]
                gv = gates[:, :, :].rearrange("p t (h b) -> p t h b", b=3)[:, :, HPG * g:HPG * g + HPG, branch]
                c = coef[:, 0, :].rearrange("p (t h) -> p t h", t=TILES)
                link(nc.vector.tensor_tensor(coef[:, 1, :].rearrange("p (t h) -> p t h", t=TILES), c, gv, ALU.mult))
                if kind == CMP:
                    c1 = coef[:, 1, :].rearrange("p (t h) -> p t h", t=TILES)
                    link(nc.vector.tensor_tensor(c1, c1, any_seen.unsqueeze(2).broadcast_to([P, TILES, HPG]), ALU.mult))

            def add_values(name, t):
                _, u, tile = name
                kind, g, _ = UNITS[u]
                if tile == 0:
                    coefficients(u)
                wait_filled(dve, t)
                src = bank[:, t.bank, :].rearrange("p (h n) -> p h n", h=HPG)
                dst = o_a[:, tile, g * 512:(g + 1) * 512].rearrange("p (h n) -> p h n", h=HPG)
                c = coef[:, 1, tile * HPG:(tile + 1) * HPG].unsqueeze(2).broadcast_to([P, HPG, HEAD])
                if kind == SLC:
                    nc.vector.tensor_tensor(dst, src, c, ALU.mult).then_inc(bank_emptied[t.bank], 1)
                    wait_moved(dve, t)
                else:
                    tmp = o_add[:, :, :]
                    nc.vector.tensor_tensor(tmp, src, c, ALU.mult).then_inc(bank_emptied[t.bank], 1)
                    wait_moved(dve, t)
                    unit_out[0] += 1
                    nc.vector.tensor_tensor(dst, dst, tmp, ALU.add).then_inc(o_ready, 1)
                    dve.wait_ge(o_ready, unit_out[0])

            def dilated_shift():
                d = [u for u, (kind, _, _) in enumerate(UNITS) if kind == DIL]
                dve.wait_ge(probs_ready, exps_before[-1])
                link(nc.vector.tensor_tensor(dilw[:, 2, 0], negmax[:, d[0], :], negmax[:, d[1], :], ALU.min))
                link(nc.vector.tensor_tensor(dilw[:, 2, 0], dilw[:, 2, 0], negmax[:, d[2], :], ALU.min))
                nc.vector.tensor_tensor(dilw[:, 0], dilw[:, 2, 0:1].broadcast_to([P, 3, 8]), negmax[:, d[0]:d[2] + 1, :],
                                        ALU.subtract).then_inc(dil_shift, 1)

            def dilated_merge():
                d = [u for u, (kind, _, _) in enumerate(UNITS) if kind == DIL]
                dve.wait_ge(dil_exp, 1)
                link(nc.vector.tensor_tensor(dilw[:, 3], dilw[:, 1], sums[:, d[0]:d[2] + 1, :], ALU.mult))
                link(nc.vector.tensor_tensor(dilw[:, 4, 0], dilw[:, 3, 0], dilw[:, 3, 1], ALU.add))
                link(nc.vector.tensor_tensor(dilw[:, 4, 0], dilw[:, 4, 0], dilw[:, 3, 2], ALU.add))
                link(nc.vector.reciprocal(dilw[:, 4, 1], dilw[:, 4, 0]))
                link(nc.vector.tensor_tensor(dilw[:, 5], dilw[:, 1], dilw[:, 4, 1:2].broadcast_to([P, 3, 8]), ALU.mult))

            def dilated_part(p_):
                d = [u for u, (kind, _, _) in enumerate(UNITS) if kind == DIL]
                for tile in range(TILES):
                    wait_moved(dve, T[("pv", d[p_], tile)])
                v = o_dil[p_].rearrange("p t (h n) -> p (t h) n", h=HPG)
                link(nc.vector.tensor_tensor(v, v, dilw[:, 5, p_].unsqueeze(2).broadcast_to([P, 8, HEAD]), ALU.mult))
                if p_ == 1:
                    link(nc.vector.tensor_tensor(o_b, o_dil[0], o_dil[1], ALU.add))
                if p_ == 2:
                    nc.vector.tensor_tensor(o_b, o_b, o_dil[2], ALU.add).then_inc(ob_ready, 1)

            last_pv = pl.at[("pv", len(UNITS) - 1, 1)] + LAG
            for pos in range(MIX_SLOTS):
                if pos >= 3:
                    split_slot(dve, mix_slot, 0, 0, pos)
                if 2 <= pos < 10:
                    x_pairs("mix", pos - 2)
                if pos == 12:
                    for v in (wg_hi[:, KT * NSA_GATES:], wg_lo[:, KT * NSA_GATES:], blk_hi[:, :, CMP_BLOCK * N_BLK:],
                              blk_lo[:, :, CMP_BLOCK * N_BLK:]):
                        nc.vector.memset(v.bitcast(F32), 0.0).then_inc(pads_zeroed, 1)
                if pos == 18:
                    dve.wait_ge(wg_rounded, 1)
                    nc.vector.tensor_tensor(wg_lo[:, 0:KT * NSA_GATES], wg_raw,
                                            wg_hi[:, 0:KT * NSA_GATES].bitcast(F32), ALU.subtract) \
                        .then_inc(wg_split, 1)
                if pos in (25, 31):
                    v = (pos - 25) // 6
                    dve.wait_ge(blk_rounded, v + 1)
                    nc.vector.tensor_tensor(blk_lo[:, v, 0:CMP_BLOCK * N_BLK], blk[:, :, :, :].rearrange("p j g n -> p (j g n)"),
                                            blk_hi[:, v, 0:CMP_BLOCK * N_BLK].bitcast(F32), ALU.subtract).then_inc(blk_split, 1)
                order, end = divmod(pos - LAG, 8)
                if end == 7 and order >= 0:
                    kind, col = MIX_ORDER[order]
                    c = mix_acc + order
                    if kind != "gate":
                        wait_acc_full(dve, mix_slot + 8 * (order + 1))
                    if kind == "cmp":
                        gx, gt = gelu_x[:, 0], gelu_x[:, 1]
                        if col:
                            wait_filled(dve, T[("hidT", 0)])
                        nc.vector.tensor_copy(gx, acc[0:N_BLK, 2 * (c % 2), 0:CMP_HIDDEN]).then_inc(acc_emptied[c % 2], 1)
                        dve.wait_ge(acc_emptied[c % 2], c // 2 + 1)
                        link(nc.vector.tensor_tensor(gt, gx, gx, ALU.mult))
                        link(nc.vector.tensor_scalar(gt, gt, 0.044715, 1.0, ALU.mult, ALU.add))
                        nc.vector.tensor_tensor(gt, gt, gx, ALU.mult).then_inc(gelu_in, 1)
                    elif kind != "gate":
                        nc.vector.tensor_copy(chunk_buf(order), acc_pair(c)).then_inc(acc_emptied[c % 2], 1)
                if pos >= LAG + 2:
                    order, end = divmod(pos - LAG - 2, 8)
                    if end == 7 and MIX_ORDER[order][0] == "cmp":
                        col = MIX_ORDER[order][1]
                        dve.wait_ge(gelu_tanh, col + 1)
                        nc.vector.scalar_tensor_tensor(gelu_x[:, 1], gelu_x[:, 1], 1.0, gelu_x[:, 0], ALU.add,
                                                       ALU.mult).then_inc(gelu_out, 1)
                for name in pl.by_pos.get(pos - LAG, ()):
                    t = T[name]
                    if name[0] == "s":
                        mask_scores(name, t)
                    elif name[0] == "pT":
                        _, u, j = name
                        wait_filled(dve, t)
                        if u:
                            wait_filled(dve, T[("pv", u - 1, 1)])
                        if UNITS[u][0] == CMP:
                            nc.vector.tensor_copy(pT[0:N_CMP, j], bank[0:N_CMP, t.bank, :]
                                                  .rearrange("p (h n) -> p h n", h=HPG)) \
                                .then_inc(bank_emptied[t.bank], 1)
                        else:
                            nc.vector.tensor_copy(pT[:, j], bank[:, t.bank, :].rearrange("p (h n) -> p h n", h=HPG)) \
                                .then_inc(bank_emptied[t.bank], 1)
                    elif name[0] == "pv" and UNITS[name[1]][0] != DIL:
                        add_values(name, t)
                    elif name[0] == "oT":
                        j = name[1]
                        split_pair(dve, name, pair_of(oT_lo, 2 * j), pair_of(oT_hi, 2 * j))
                    elif name[0] == "gatesT":
                        wait_filled(dve, t)
                        nc.vector.tensor_scalar(gates[:, :, :], bank[:, t.bank, 0:TILES * NSA_GATES]
                                                .rearrange("p (t n) -> p t n", t=TILES), 0.5, 0.5, ALU.mult, ALU.add) \
                            .then_inc(bank_emptied[t.bank], 1)
                        wait_moved(dve, t)
                if pos in max_at:
                    maxima(max_at[pos])
                if pos - 2 in max_at and UNITS[max_at[pos - 2]][0] == CMP:
                    u = max_at[pos - 2]
                    dve.wait_ge(probs_ready, exps_before[u + 1])
                    v = s0[:, 0, 0:8 * N_CMP].rearrange("p (e n) -> p e n", e=8)
                    link(nc.vector.tensor_reduce(sums[:, u, :], v, AX_X, ALU.add))
                if pos == last_pv + 1:
                    dilated_shift()
                if pos == last_pv + 3:
                    dilated_merge()
                if last_pv + 4 <= pos < last_pv + 7:
                    dilated_part(pos - last_pv - 4)

            def merge_a(n):
                ca = ab_acc + 2 * n
                dve.wait_ge(slots_used, tail_slot + 6 * n + 4)
                if n == 0:
                    dve.wait_ge(acc_emptied[(mix_acc + len(MIX_ORDER) - 1) % 2], (mix_acc + len(MIX_ORDER) - 1) // 2 + 1)
                nc.vector.scalar_tensor_tensor(rot_tmp[:, :, :], chunk_buf(first_gate + n), 1.0, acc_pair(ca), ALU.add,
                                               ALU.mult).then_inc(acc_emptied[0], 1)

            def merge_b(n):
                ca, cb = ab_acc + 2 * n, ab_acc + 2 * n + 1
                v_ = (rot_q, rot_k)[n % 2]
                dve.wait_ge(slots_used, tail_slot + 6 * (n + 1))
                if n >= 2:
                    wait_filled(dve, T[("m", n - 2, 1)])
                nc.vector.scalar_tensor_tensor(v_[:, :, :], chunk_buf(first_gate + 4 + n), 1.0, acc_pair(cb), ALU.add,
                                               ALU.mult).then_inc(acc_emptied[1], 1)
                dve.wait_ge(acc_emptied[0], ca // 2 + 1)
                dve.wait_ge(acc_emptied[1], cb // 2 + 1)
                nc.vector.tensor_tensor(v_[:, :, :], rot_tmp[:, :, :], v_[:, :, :], ALU.add).then_inc(merged, 1)
                dve.wait_ge(merged, n + 1)

            first_gate = len(MIX_ORDER) - 8
            for pos in range(TAIL_SLOTS):
                split_slot(dve, tail_slot, 0, 0, pos)
                if pos >= LAG and (pos - LAG) // 6 < OUT_CHUNKS:
                    if (pos - LAG) % 6 == 3:
                        merge_a((pos - LAG) // 6)
                    if (pos - LAG) % 6 == 5:
                        merge_b((pos - LAG) // 6)
                for d in range(2):
                    if pos - LAG - d in merge_at:
                        n = merge_at[pos - LAG - d]
                        kt = 4 * n + 2 * d
                        split_pair(dve, ("m", n, d), pair_of(act_lo, kt), pair_of(act_hi, kt), 0.5)
                o_pos = pos - 6 * OUT_CHUNKS - LAG
                if o_pos >= 0 and o_pos % 8 == 7:
                    c = o_pos // 8
                    if c == 0:
                        dve.wait_ge(resid_ready, 2)
                    add_chunk_static(c)

            for s in range(3):
                split_slot(dve, gu_slot[1], 0, 0, s)
            add_chunk_static(OUT_CHUNKS - 1)
            layer_norm(1)
            gu_chunk(1, 0, True)
            with dve.Fori(1, GU_CHUNKS) as i:
                gu_chunk(1, i, False)
            up_half(1, GU_CHUNKS)
            for s in range(3):
                split_slot(dve, down_slot[1], 0, 0, s)
            for half in range(2):
                split_h(1, GU_CHUNKS, half)
            down(1)
            last_chunk_tile(0)
            dve.wait_ge(ln_nat_loaded, 3 * 32)
            v = resid[:, 0, 1024:2048]
            link(nc.vector.scalar_tensor_tensor(v, v, mv[:, 0, 0:1], ln_nat[:, 0, 1024:2048], ALU.subtract, ALU.mult))
            last_chunk_tile(1)
            nc.vector.scalar_tensor_tensor(v, v, ln_s[:, 3, 0:1], ln_nat[:, 1, 1024:2048], ALU.mult, ALU.add) \
                .then_inc(out_ready, 1)
            for n, (lo, hi) in enumerate(OUT_PIECES[2:]):
                dve.wait_ge(z_act, 6 + 3 + n)
                v = resid[:, 1, lo:hi]
                link(nc.vector.tensor_tensor(v, v, ln_nat[:, 0, lo:hi], ALU.mult))
                nc.vector.tensor_tensor(v, v, ln_nat[:, 1, lo:hi], ALU.add).then_inc(out_ready, 1)

        @block.tensor
        def _(pe):
            def x_task(f, j):
                t = T[("x", f, j)]
                if f == 0:
                    if j == 0:
                        pe.wait_ge(small_loaded, 16)
                    if j % 2 == 0:
                        pe.wait_ge(x_loaded[j // 2], 16)
                else:
                    ln = 2 if f == 1 else 1
                    if 2 * P * j in (lo for lo, _ in Z_PIECES):
                        piece = [lo for lo, _ in Z_PIECES].index(2 * P * j) + 1
                        pe.wait_ge(z_dve, 3 * (ln - 1) + piece)
                        pe.wait_ge(z_act, 3 * (ln - 1) + piece)
                wait_bank_free(pe, t)
                transpose_pair(resid, 2 * P * j, t.bank)

            def keep_warm(n, b, a=ident, v=act_hi[:, 0:2, :].bitcast(F32)):
                for _ in range(n):
                    nc.tensor.matmul(bank[:, b, :], a, v, start=True, stop=True)

            def first_chunk(f, n0, c0):
                wait_acc_free(pe, c0, 0, 2, 0)
                if f:
                    wait_bank_free(pe, T[("x", f, 3)])
                    keep_warm(WARM_LN, 3)
                else:
                    pe.wait_ge(zeros_ready, 1)
                    keep_warm(WARM_START, 3, hid[:, 0, 0:P], hid[:, 0, :])
                lead = 3 if f else 2
                for j in range(lead):
                    x_task(f, j)
                for s in range(GU_SLOTS):
                    if s + lead < GU_SLOTS:
                        x_task(f, s + lead)
                    input_ready(f, s)
                    multiply_slot(pe, act_hi, act_lo, 2 * s, c0 % 2, s == 0, s == GU_SLOTS - 1, n0, 0, 0, s)

            def input_ready(f, j):
                t = T[("x", f, j)]
                if f == 0:
                    wait_moved(pe, t)
                else:
                    pe.wait_ge(lo_pairs, (0 if f == "mix" else 8) + j + 1)

            def h_task(f, i, half):
                t = T[("h", f, 0, half)]
                if half == 0:
                    pe.wait_ge(acc_emptied[1], i + (gu_acc[f] // 2))
                if not (isinstance(i, int) and i - 1 + t.use == 0):
                    pe.wait_ge(bank_emptied[half], i + (t.use - 1))
                transpose_pair(hid, 2 * P * half, half)

            def gu_chunk(f, i, peel):
                n0, per, c0 = gu_slot[f], 2 * GU_SLOTS, gu_acc[f]
                for h in range(2):
                    if peel and h == 0:
                        first_chunk(f, n0, c0)
                        if f == 0:
                            setup_task()
                        continue
                    wait_acc_free(pe, c0, i, 2, h)
                    for s in range(GU_SLOTS):
                        multiply_slot(pe, act_hi, act_lo, 2 * s, h, s == 0, s == GU_SLOTS - 1, n0, i, per,
                                      h * GU_SLOTS + s)
                        if not peel and h == 0 and s in (3, 4):
                            h_task(f, i, s - 3)

            def setup_task():
                t = T[("setup",)]
                pe.wait_ge(consts_loaded, 16 * 6)
                wait_bank_free(pe, t)
                nc.tensor.transpose(bank[:, t.bank, 0:64], vec_rows[:, :], ident[0:64, 0:64])
                nc.tensor.transpose(bank[:, t.bank, 64:96], pos_rows[:, 0, :], ident[0:32, 0:32])
                nc.tensor.transpose(bank[:, t.bank, 96:128], pos_rows[:, 1, :], ident[0:32, 0:32]).then_inc(bank_filled, 1)

            def ffn(f):
                gu_chunk(f, 0, True)
                with pe.Fori(1, GU_CHUNKS) as i:
                    gu_chunk(f, i, False)
                for half in range(2):
                    h_task(f, GU_CHUNKS, half)
                wait_moved(pe, T[("setup",) if f == 0 else ("x", 1, 6)])
                keep_warm(WARM_H, 2)
                for half in range(2):
                    wait_moved(pe, T[("h", f, GU_CHUNKS - 1, half)])
                with pe.Fori(0, 2) as i:
                    for c in range(2):
                        wait_acc_free(pe, down_acc[f], i, 2, c)
                        whole = DOWN_SLOTS - RING * f
                        steps = [(s, range(TILES)) for s in range(whole)]
                        steps += [(s, (tile,)) for tile in range(TILES) for s in range(whole, DOWN_SLOTS)]
                        for s, tiles in steps:
                            multiply_slot(pe, hT_hi, hT_lo, 2 * s, (down_acc[f] + c) % 2, s == 0, s == DOWN_SLOTS - 1,
                                          down_slot[f], i, 2 * DOWN_SLOTS, c * DOWN_SLOTS + s, tiles)

            ffn(0)

            def buffered(eng_order):
                c = mix_acc + eng_order
                pe.wait_ge(acc_emptied[c % 2], c // 2 + 1)

            def heads_T(src, t):
                wait_bank_free(pe, t)
                for h, v in enumerate(src):
                    mm = nc.tensor.transpose(bank[:, t.bank, h * P:(h + 1) * P], v, ident)
                mm.then_inc(bank_filled, 1)

            def gate_products(t):
                pe.wait_ge(wg_split, 1)
                pe.wait_ge(pads_zeroed, 4)
                wait_bank_free(pe, t)
                o = bank[0:WIDE, t.bank, 0:TOKENS]
                for k in range(KT):
                    hi, lo = (w[:, k * NSA_GATES:k * NSA_GATES + WIDE] for w in (wg_hi, wg_lo))
                    nc.tensor.matmul(o, hi, act_hi[:, k, :], start=k == 0, stop=False)
                    nc.tensor.matmul(o, hi, act_lo[:, k, :], start=False, stop=False)
                    mm = nc.tensor.matmul(o, lo, act_hi[:, k, :], start=False, stop=k == KT - 1)
                mm.then_inc(bank_filled, 1)

            def gates_back(t):
                wait_moved(pe, T[("gates",)])
                wait_bank_free(pe, t)
                for tile in range(TILES):
                    mm = nc.tensor.transpose(bank[:, t.bank, tile * NSA_GATES:(tile + 1) * NSA_GATES],
                                             gatesT[:, tile * P:(tile + 1) * P], ident[0:NSA_GATES, 0:NSA_GATES])
                mm.then_inc(bank_filled, 1)

            def cmp_hidden(v, t):
                pe.wait_ge(gelu_out, v + 1)
                wait_bank_free(pe, t)
                for k in range(2):
                    mm = nc.tensor.transpose(bank[:, t.bank, k * N_BLK:(k + 1) * N_BLK], gelu_x[:, 1, k * P:(k + 1) * P],
                                             ident[0:N_BLK, 0:N_BLK])
                mm.then_inc(bank_filled, 1)

            def cmp_out(name, t):
                v = int(name[0] == "vcmp")
                wait_moved(pe, T[("hidT", v)])
                pe.wait_ge(cw2_loaded, 32)
                wait_bank_free(pe, t)
                if v == 0:
                    for k in range(2):
                        mm = nc.tensor.matmul(bank[:, t.bank, 0:N_BLK], cw2[:, 0, k, :], hidT[:, 0, k, :],
                                              start=k == 0, stop=k == 1)
                else:
                    for g in range(GROUPS):
                        for k in range(2):
                            mm = nc.tensor.matmul(bank[0:N_CMP, t.bank, g * HEAD:(g + 1) * HEAD],
                                                  hidT[:, 1, k, g * N_CMP:(g + 1) * N_CMP], cw2[:, 1, k, :],
                                                  start=k == 0, stop=k == 1)
                mm.then_inc(bank_filled, 1)

            def queries(name, t):
                _, u, tile = name
                kind, g, _ = UNITS[u]
                if kind == CMP:
                    buffered(3 + g)
                    src = chunk_buf(3 + g)
                else:
                    pe.wait_ge(roped, 2 + g if kind == SLC else 4 + 2 * g)
                    src = rot_q
                heads_T([src[:, tile, h * HEAD:(h + 1) * HEAD] for h in range(HPG)], t)

            def keys(name, t):
                _, u, tile = name
                kind, g, _ = UNITS[u]
                pe.wait_ge(roped, 1 if kind == SLC else 5 + 2 * g)
                heads_T([rot_k[:, tile, h * HEAD:(h + 1) * HEAD] for h in range(HPG)], t)

            def scores(name, t):
                _, u, j = name
                kind, g, _ = UNITS[u]
                owner = u - 1 if kind == WINDOW else u
                for tile in range(TILES):
                    wait_moved(pe, T[("qT", owner, tile)])
                if kind in (SLC, WINDOW):
                    for tile in range(TILES):
                        wait_moved(pe, T[("kT", 0, tile)])
                if kind == DIL:
                    for tile in range(TILES):
                        wait_moved(pe, T[("kT", u, tile)])
                if kind == CMP:
                    wait_moved(pe, T[("kcmp",)])
                wait_bank_free(pe, t)

                def key(h, lo, hi):
                    if kind == DIL:
                        return kT[:, h, lo:hi]
                    return kT[:, (0 if kind == SLC else 2) + g, lo:hi]

                if kind == CMP:
                    for tile in range(TILES):
                        for h in range(HPG):
                            e = tile * HPG + h
                            mm = nc.tensor.matmul(bank[:, t.bank, e * N_CMP:(e + 1) * N_CMP], qT[:, h, tile * P:(tile + 1) * P],
                                                  kcmpT[:, g * N_CMP:(g + 1) * N_CMP], start=True, stop=True)
                elif j < 2:
                    for h in range(2 * j, 2 * j + 2):
                        o = (h - 2 * j) * TOKENS
                        mm = nc.tensor.matmul(bank[:, t.bank, o:o + TOKENS], qT[:, h, P:TOKENS], key(h, 0, TOKENS),
                                              start=True, stop=True)
                else:
                    for h in range(HPG):
                        mm = nc.tensor.matmul(bank[:, t.bank, h * P:(h + 1) * P], qT[:, h, 0:P], key(h, 0, P),
                                              start=True, stop=True)
                mm.then_inc(bank_filled, 1)

            def probs_T(name, t):
                _, u, j = name
                pe.wait_ge(probs_ready, exps_before[u + 1])
                wait_bank_free(pe, t)
                if UNITS[u][0] == CMP:
                    for h in range(HPG):
                        e = j * HPG + h
                        mm = nc.tensor.transpose(bank[0:N_CMP, t.bank, h * P:(h + 1) * P],
                                                 s0[:, 0, e * N_CMP:(e + 1) * N_CMP], ident)
                else:
                    for h in range(HPG):
                        v = s1[:, h, j * P:(j + 1) * P] if j < 2 else s0[:, h, :]
                        mm = nc.tensor.transpose(bank[:, t.bank, h * P:(h + 1) * P], v, ident)
                mm.then_inc(bank_filled, 1)

            def values(name, t):
                _, u, tile = name
                kind, g, _ = UNITS[u]
                for j in range(2 if kind == CMP else 3):
                    wait_moved(pe, T[("pT", u, j)])
                if kind == CMP:
                    wait_moved(pe, T[("vcmp",)])
                elif kind == DIL:
                    buffered(9 + 3 * g)
                else:
                    buffered(1 if kind == SLC else 2)
                wait_bank_free(pe, t)
                for h in range(HPG):
                    o = bank[:, t.bank, h * P:(h + 1) * P]
                    if kind == CMP:
                        mm = nc.tensor.matmul(o, pT[0:N_CMP, tile, h, :], vcmp[:, g, :], start=True, stop=True)
                        continue
                    if kind == DIL:
                        v, c0 = chunk_buf(9 + 3 * g), h * HEAD
                    else:
                        v, c0 = chunk_buf(1 if kind == SLC else 2), 256 + g * HEAD
                    parts = [(2, 0)] if tile == 0 else [(0, 0), (1, 1)]
                    for n, (j, kt) in enumerate(parts):
                        mm = nc.tensor.matmul(o, pT[:, j, h, :], v[:, kt, c0:c0 + HEAD], start=n == 0,
                                              stop=n == len(parts) - 1)
                mm.then_inc(bank_filled, 1)

            def bank_task(name):
                t = T[name]
                if name[0] == "kcT" or name[0] == "vcT":
                    buffered(0)
                    wait_bank_free(pe, t)
                    transpose_pair(chunk_buf(0), 256 * int(name[0] == "vcT"), t.bank)
                elif name[0] == "gates":
                    gate_products(t)
                elif name[0] == "gatesT":
                    gates_back(t)
                elif name[0] == "hidT":
                    cmp_hidden(name[1], t)
                elif name[0] in ("kcmp", "vcmp"):
                    cmp_out(name, t)
                elif name[0] == "qT":
                    queries(name, t)
                elif name[0] == "kT":
                    keys(name, t)
                elif name[0] == "s":
                    scores(name, t)
                elif name[0] == "pT":
                    probs_T(name, t)
                elif name[0] == "pv":
                    values(name, t)
                elif name[0] == "oT":
                    j = name[1]
                    if j < 4:
                        pe.wait_ge(o_ready, 8)
                    else:
                        pe.wait_ge(ob_ready, 1)
                    wait_bank_free(pe, t)
                    if j < 4:
                        transpose_pair(o_a, 2 * P * j, t.bank)
                    else:
                        transpose_pair(o_b, 2 * P * (j - 4), t.bank)

            def cmp_slot(v, s, n, pair):
                r = n % RING
                pe.wait_ge(lo_done, n + 1)
                o = acc[0:WIDE, 2 * pair, 0:CMP_HIDDEN]
                for k in range(4):
                    j = (4 * s + k) * N_BLK
                    b_hi, b_lo = blk_hi[:, v, j:j + WIDE], blk_lo[:, v, j:j + WIDE]
                    first, last = s == 0 and k == 0, s == CMP_SLOTS - 1 and k == 3
                    hi, lo = (w[:, r, k * CMP_HIDDEN:(k + 1) * CMP_HIDDEN] for w in (w_hi, w_lo))
                    nc.tensor.matmul(o, b_hi, hi, start=first, stop=False)
                    nc.tensor.matmul(o, b_hi, lo, start=False, stop=False)
                    mm = nc.tensor.matmul(o, b_lo, hi, start=False, stop=last)
                mm.then_inc(slots_used, 1)

            for order, (kind, col) in enumerate(MIX_ORDER):
                c = mix_acc + order
                if order:
                    wait_acc_free(pe, c, 0, 2, 0)
                if kind == "cmp":
                    pe.wait_ge(blk_split, col + 1)
                for s in range(8):
                    pos = 8 * order + s
                    if order == 0:
                        if s == 0:
                            wait_bank_free(pe, T[("x", "mix", 3)])
                            keep_warm(WARM_LN, 3)
                            wait_acc_free(pe, c, 0, 2, 0)
                            for j in range(3):
                                x_task("mix", j)
                        if s + 3 < GU_SLOTS:
                            x_task("mix", s + 3)
                        input_ready("mix", s)
                    if kind == "cmp":
                        cmp_slot(col, s, mix_slot + pos, c % 2)
                    else:
                        multiply_slot(pe, act_hi, act_lo, 2 * s, c % 2, s == 0, s == 7, mix_slot, 0, 0, pos)
                    for name in pl.by_pos.get(pos, ()):
                        bank_task(name)

            def merge_tasks(pos):
                for d in range(2):
                    if pos - d in merge_at:
                        n = merge_at[pos - d]
                        t = T[("m", n, d)]
                        if d == 0:
                            pe.wait_ge(merged, n + 1)
                        wait_bank_free(pe, t)
                        transpose_pair((rot_q, rot_k)[n % 2], 2 * P * d, t.bank)

            pos = 0
            for n in range(OUT_CHUNKS):
                for part, (ns, kt0) in enumerate(((4, 0), (2, 8))):
                    c = ab_acc + 2 * n + part
                    wait_acc_free(pe, c, 0, 2, 0)
                    if n == 0:
                        for j in (range(4) if part == 0 else range(4, 6)):
                            wait_moved(pe, T[("oT", j)])
                    for s in range(ns):
                        multiply_slot(pe, oT_hi, oT_lo, kt0 + 2 * s, c % 2, s == 0, s == ns - 1, tail_slot, 0, 0, pos)
                        merge_tasks(pos)
                        pos += 1
            for n in range(OUT_CHUNKS):
                c = o_acc + n
                wait_acc_free(pe, c, 0, 2, 0)
                for s in range(8):
                    if n == 0:
                        wait_moved(pe, T[("m", s // 2, s % 2)])
                    multiply_slot(pe, act_hi, act_lo, 2 * s, c % 2, s == 0, s == 7, tail_slot, 0, 0, pos)
                    merge_tasks(pos)
                    pos += 1

            ffn(1)

        @block.gpsimd
        def _(pool):
            steps = [0]

            def link(ins):
                steps[0] += 1
                ins.then_inc(pool_step, 1)
                pool.wait_ge(pool_step, steps[0])

            def residual(which):
                wait_filled(pool, T[("x", 0, 7) if which == 0 else ("x", "mix", 7) if which == 1 else ("x", 1, 7)])
                if which == 0:
                    nc.gpsimd.tensor_scalar(resid[:, :, :], resid[:, :, :], ALPHA, None, ALU.mult).then_inc(resid_ready, 1)
                    return
                pool.wait_ge(ln_nat_loaded, 32 * which)
                link(nc.gpsimd.tensor_scalar(ln_nat[:, :, :], ln_nat[:, :, :], ALPHA, None, ALU.mult))
                for tile in range(TILES):
                    link(nc.gpsimd.tensor_tensor(resid[:, tile, :], resid[:, tile, :], ln_nat[:, 0, :], ALU.mult))
                link(nc.gpsimd.tensor_tensor(resid[:, 0, :], resid[:, 0, :], ln_nat[:, 1, :], ALU.add))
                nc.gpsimd.tensor_tensor(resid[:, 1, :], resid[:, 1, :], ln_nat[:, 1, :], ALU.add).then_inc(resid_ready, 1)

            def rotate(src, dst, tmp, heads):
                cos = rope[:, 0].unsqueeze(2).broadcast_to([P, TILES, heads, HEAD])
                sin_a = rope[:, 1, :, 0:64].unsqueeze(2).broadcast_to([P, TILES, heads, 64])
                sin_b = rope[:, 1, :, 64:128].unsqueeze(2).broadcast_to([P, TILES, heads, 64])
                s_, d_, t_ = (v.rearrange("p t (h n) -> p t h n", n=HEAD) for v in (src, dst, tmp))
                link(nc.gpsimd.tensor_tensor(t_[:, :, :, 0:64], s_[:, :, :, 64:128], sin_a, ALU.mult))
                link(nc.gpsimd.tensor_tensor(t_[:, :, :, 64:128], s_[:, :, :, 0:64], sin_b, ALU.mult))
                link(nc.gpsimd.tensor_tensor(d_, s_, cos, ALU.mult))
                return d_, t_

            def projected(order):
                c = mix_acc + order
                pool.wait_ge(acc_emptied[c % 2], c // 2 + 1)

            jobs = [0]

            def rotate_job(parts, dst, readers):
                for r in readers:
                    wait_filled(pool, T[r])
                at = 0
                for n, (order, lo, hi) in enumerate(parts):
                    projected(order)
                    w = hi - lo
                    d_, t_ = rotate(chunk_buf(order)[:, :, lo:hi], dst[:, :, at:at + w], rot_tmp[:, :, at:at + w], w // HEAD)
                    ins = nc.gpsimd.tensor_tensor(d_, d_, t_, ALU.add)
                    if n < len(parts) - 1:
                        link(ins)
                    at += w
                ins.then_inc(roped, 1)
                jobs[0] += 1
                pool.wait_ge(roped, jobs[0])

            residual(0)
            residual(1)
            for v in range(2):
                wait_moved(pool, T[("kcT",) if v == 0 else ("vcT",)])
                if v:
                    pool.wait_ge(blk_split, 1)
                for g in range(GROUPS):
                    windows = kcvcT[:, v, g, :].rearrange("p (m r) -> p r m", r=CMP_STRIDE)
                    for a in range(2):
                        js = slice(16 * a, 16 * a + 16)
                        ins = nc.gpsimd.tensor_tensor(
                            blk[:, js, g, :], windows[:, :, a:a + N_CMP],
                            posT[:, v, js].unsqueeze(2).broadcast_to([P, 16, N_CMP]), ALU.add)
                        if (g, a) != (1, 1):
                            link(ins)
                ins.then_inc(blk_ready, 1)
            pool.wait_ge(mix_consts_loaded, 48)
            rotate_job([(1, 0, 256), (2, 0, 256)], rot_k, [])
            rotate_job([(3, 0, 512)], rot_q, [])
            rotate_job([(4, 0, 512)], rot_q, [("qT", 0, 1)])
            for p_ in range(3):
                u = 6 + p_
                prev_q = ("qT", 2, 1) if p_ == 0 else ("qT", u - 1, 1)
                prev_k = ("kT", 0, 1) if p_ == 0 else ("kT", u - 1, 1)
                rotate_job([(7 + 3 * p_, 0, 512)], rot_q, [prev_q])
                rotate_job([(8 + 3 * p_, 0, 512)], rot_k, [prev_k])
            residual(2)
            pool.wait_ge(ln_nat_loaded, 96)
            for tile, (lo, hi) in enumerate(OUT_PIECES[:2]):
                pool.wait_ge(z_act, 6 + 1 + tile)
                v = resid[:, tile, lo:hi]
                link(nc.gpsimd.tensor_tensor(v, v, ln_nat[:, 0, lo:hi], ALU.mult))
                nc.gpsimd.tensor_tensor(v, v, ln_nat[:, 1, lo:hi], ALU.add).then_inc(out_ready_pool, 1)


_INS = ["x", "ffn1_w_gate", "ffn1_w_up", "ffn1_w_down", "ln_ffn1_g", "ln_ffn1_b", "w_in", "cmp_k_pos", "cmp_k_w1",
        "cmp_k_w2", "cmp_v_pos", "cmp_v_w1", "cmp_v_w2", "w_branch_a", "w_branch_b", "w_o", "ln_mix_g", "ln_mix_b",
        "ffn2_w_gate", "ffn2_w_up", "ffn2_w_down", "ln_ffn2_g", "ln_ffn2_b"]


def kernel(**inputs):
    import concourse.bacc as bacc
    from concourse.bass_utils import run_bass_kernel_spmd

    nc = bacc.Bacc("TRN2", target_bir_lowering=False, num_devices=1, dynamic_dma_scratch_size=1024)
    named = [(name, np.ascontiguousarray(inputs[name])) for name in _INS]
    named += list(zip(("rope", "masks", "small"), mixer_constants()))
    arrays, args = {}, []
    for name, a in named:
        arrays[f"in_{name}_dram"] = a
        args.append(nc.dram_tensor(f"in_{name}_dram", a.shape, mybir.dt.from_np(a.dtype), kind="ExternalInput").ap())
    out = nc.dram_tensor("out_dram", (1, TOKENS, D), F32, kind="ExternalOutput").ap()
    build(nc, *args, out)
    r = run_bass_kernel_spmd(nc, [arrays], core_ids=[0])
    return r.results[0]["out_dram"]
```
